# Optimizing a Trainium2 kernel written in Bass

```python
import jax
import jax.numpy as jnp
from jax import lax
import numpy as np

D_MODEL = 1024
BATCH = 1
SEQ = 2048
DEPTH = 1
DEC_BATCH = 8
DEC_SEQ = 8
PAST_LEN = 4096
PAGE_SIZE = 128

HEAD_DIM = 64
N_HEADS = D_MODEL // HEAD_DIM
SWA_HEADS = N_HEADS // 2
GDN_HEADS = N_HEADS - SWA_HEADS
SWA_KV_HEADS = 2
GQA_GROUP = SWA_HEADS // SWA_KV_HEADS
WINDOW = 128
ATTN_SCALE = HEAD_DIM ** -0.5
GDN_DK = HEAD_DIM
GDN_DV = HEAD_DIM
CONV_W = 4
GDN_CHUNK = 64
N_GROUPS = 8
EXPERTS_PER_GROUP = 8
N_EXPERTS = N_GROUPS * EXPERTS_PER_GROUP
TOP_K_IN_GROUP = 2
D_EXPERT = D_MODEL // 4
MOE_BLOCK = 128
EPS = 1e-6

SWA_Q = SWA_HEADS * HEAD_DIM
SWA_KV = SWA_KV_HEADS * HEAD_DIM
GDN_QK = GDN_HEADS * GDN_DK
GDN_V = GDN_HEADS * GDN_DV
GDN_CONV_CH = 2 * GDN_QK + GDN_V
D_MIX = SWA_Q + GDN_V
IN_SPLITS = (SWA_Q,
             SWA_Q + SWA_KV,
             SWA_Q + 2 * SWA_KV,
             SWA_Q + 2 * SWA_KV + GDN_CONV_CH,
             SWA_Q + 2 * SWA_KV + GDN_CONV_CH + GDN_V,
             SWA_Q + 2 * SWA_KV + GDN_CONV_CH + GDN_V + GDN_HEADS)
D_IN = SWA_Q + 2 * SWA_KV + GDN_CONV_CH + GDN_V + 2 * GDN_HEADS

kernel_name = 'hymba_swa_sink_gdn_hier_moe_step'

def rmsnorm(x, g):
    xf = x.astype(jnp.float32)
    y = xf * lax.rsqrt(jnp.mean(xf * xf, axis=-1, keepdims=True) + EPS)
    return (y * g.astype(jnp.float32)).astype(x.dtype)

def l2norm(x):
    return x * lax.rsqrt(jnp.sum(x * x, axis=-1, keepdims=True) + EPS)

def sink_softmax(s, sink):
    m = jnp.maximum(jnp.max(s, axis=-1, keepdims=True), sink)
    p = jnp.exp(s - m)
    return p / (jnp.sum(p, axis=-1, keepdims=True) + jnp.exp(sink - m))

def swa_prompt(q, k, v, sinks):
    B, S = q.shape[0], q.shape[1]
    nb = S // WINDOW
    qb = q.reshape(B, nb, WINDOW, SWA_KV_HEADS, GQA_GROUP, HEAD_DIM)
    kb = k.reshape(B, nb, WINDOW, SWA_KV_HEADS, HEAD_DIM)
    vb = v.reshape(B, nb, WINDOW, SWA_KV_HEADS, HEAD_DIM)
    pad = ((0, 0), (1, 0), (0, 0), (0, 0), (0, 0))
    kk = jnp.concatenate([jnp.pad(kb, pad)[:, :-1], kb], axis=2)
    vv = jnp.concatenate([jnp.pad(vb, pad)[:, :-1], vb], axis=2)
    s = jnp.einsum('bnqhgd,bnkhd->bnhgqk', qb, kk, preferred_element_type=jnp.float32) * ATTN_SCALE
    qi = WINDOW + jnp.arange(WINDOW)[:, None]
    kj = jnp.arange(2 * WINDOW)[None, :]
    band = (kj <= qi) & (qi - kj < WINDOW)
    has_prev = (jnp.arange(nb) > 0)[:, None, None] | (kj >= WINDOW)[None]
    mask = band[None] & has_prev
    s = jnp.where(mask[None, :, None, None], s, -jnp.inf)
    p = sink_softmax(s, sinks.astype(jnp.float32).reshape(SWA_KV_HEADS, GQA_GROUP, 1, 1))
    o = jnp.einsum('bnhgqk,bnkhd->bnqhgd', p.astype(vv.dtype), vv)
    return o.reshape(B, S, SWA_Q)

def swa_sample(q, k, v, k_buf, v_buf, sinks):
    Bd, T = q.shape[0], q.shape[1]
    Wb = k_buf.shape[1]
    kk = jnp.concatenate([k_buf.astype(k.dtype), k.reshape(Bd, T, SWA_KV_HEADS, HEAD_DIM)], axis=1)
    vv = jnp.concatenate([v_buf.astype(v.dtype), v.reshape(Bd, T, SWA_KV_HEADS, HEAD_DIM)], axis=1)
    qg = q.reshape(Bd, T, SWA_KV_HEADS, GQA_GROUP, HEAD_DIM)
    s = jnp.einsum('bqhgd,bkhd->bhgqk', qg, kk, preferred_element_type=jnp.float32) * ATTN_SCALE
    qpos = Wb + jnp.arange(T)[:, None]
    kpos = jnp.arange(Wb + T)[None, :]
    mask = (kpos <= qpos) & (qpos - kpos < WINDOW)
    s = jnp.where(mask, s, -jnp.inf)
    p = sink_softmax(s, sinks.astype(jnp.float32).reshape(SWA_KV_HEADS, GQA_GROUP, 1, 1))
    o = jnp.einsum('bhgqk,bkhd->bqhgd', p.astype(vv.dtype), vv)
    return o.reshape(Bd, T, SWA_Q), kk[:, -Wb:], vv[:, -Wb:]

def causal_short_conv(x_ext, w):
    T = x_ext.shape[1] - (CONV_W - 1)
    out = x_ext[:, 0:T] * w[0]
    for i in range(1, CONV_W):
        out = out + x_ext[:, i:i + T] * w[i]
    return jax.nn.silu(out)

def chunked_gated_delta(q, k, v, g, beta, S0):
    B, T, H, dk = q.shape
    dv = v.shape[-1]
    C = GDN_CHUNK
    n = -(-T // C)
    pad = n * C - T

    def blocks(x):
        x = jnp.pad(x, [(0, 0), (0, pad)] + [(0, 0)] * (x.ndim - 2))
        x = x.reshape((B, n, C) + x.shape[2:])
        return jnp.moveaxis(x, (1, 3), (0, 2))

    qc, kc, vc, bc = blocks(q), blocks(k), blocks(v), blocks(beta)
    gc = jnp.cumsum(blocks(g), axis=-1)
    causal = jnp.tril(jnp.ones((C, C), bool))
    strict = jnp.tril(jnp.ones((C, C), bool), -1)
    decay = jnp.exp(jnp.where(causal, gc[..., :, None] - gc[..., None, :], -jnp.inf))
    kb = kc * bc[..., None]
    L = jnp.where(strict, jnp.einsum('nbhcd,nbhjd->nbhcj', kb, kc) * decay, 0.0)
    A = L + jnp.eye(C, dtype=L.dtype)
    rhs = jnp.concatenate([vc * bc[..., None], kb * jnp.exp(gc)[..., None]], axis=-1)
    sol = lax.linalg.triangular_solve(A, rhs, left_side=True, lower=True, unit_diagonal=True)
    u, w = sol[..., :dv], sol[..., dv:]
    qk = jnp.einsum('nbhcd,nbhjd->nbhcj', qc, kc) * decay
    q_dec = qc * jnp.exp(gc)[..., None]
    k_dec = kc * jnp.exp(gc[..., -1:] - gc)[..., None]
    g_tot = jnp.exp(gc[..., -1])

    def step(S, xs):
        u_c, w_c, qk_c, qd_c, kd_c, gt_c = xs
        v_new = u_c - jnp.einsum('bhcd,bhdv->bhcv', w_c, S)
        o_c = jnp.einsum('bhcd,bhdv->bhcv', qd_c, S) + jnp.einsum('bhcj,bhjv->bhcv', qk_c, v_new)
        S = S * gt_c[..., None, None] + jnp.einsum('bhcd,bhcv->bhdv', kd_c, v_new)
        return S, o_c

    S_fin, o = lax.scan(step, S0, (u, w, qk, q_dec, k_dec, g_tot))
    o = jnp.moveaxis(o, (0, 2), (1, 3)).reshape(B, n * C, H, dv)[:, :T]
    return o, S_fin

def gated_deltanet(c, z, a, b, S0, A_log, dt_bias, norm_w):
    B, T = c.shape[0], c.shape[1]
    cf = c.astype(jnp.float32)
    q = l2norm(cf[..., :GDN_QK].reshape(B, T, GDN_HEADS, GDN_DK)) * (GDN_DK ** -0.5)
    k = l2norm(cf[..., GDN_QK:2 * GDN_QK].reshape(B, T, GDN_HEADS, GDN_DK))
    v = cf[..., 2 * GDN_QK:].reshape(B, T, GDN_HEADS, GDN_DV)
    beta = jax.nn.sigmoid(b.astype(jnp.float32))
    g = -jnp.exp(A_log.astype(jnp.float32)) * jax.nn.softplus(a.astype(jnp.float32) + dt_bias.astype(jnp.float32))
    o, S = chunked_gated_delta(q, k, v, g, beta, S0.astype(jnp.float32))
    o = o * lax.rsqrt(jnp.mean(o * o, axis=-1, keepdims=True) + EPS) * norm_w.astype(jnp.float32)
    o = o * jax.nn.silu(z.astype(jnp.float32).reshape(B, T, GDN_HEADS, GDN_DV))
    return o.reshape(B, T, GDN_V).astype(c.dtype), S

def routed_expert_mlps(x, expert_ids, gates, w_gate, w_up, w_down):
    N, D = x.shape
    A = expert_ids.shape[0] * expert_ids.shape[1]
    e_flat = expert_ids.reshape(A)
    tok_flat = jnp.arange(A, dtype=jnp.int32) // TOP_K_IN_GROUP
    g_flat = gates.reshape(A)
    order = jnp.argsort(e_flat)
    e_s, tok_s, g_s = e_flat[order], tok_flat[order], g_flat[order]
    counts = jnp.zeros((N_EXPERTS,), jnp.int32).at[e_flat].add(1)
    start = jnp.cumsum(counts) - counts
    padded = (counts + MOE_BLOCK - 1) // MOE_BLOCK * MOE_BLOCK
    p_end = jnp.cumsum(padded)
    dest = (p_end - padded)[e_s] + (jnp.arange(A, dtype=jnp.int32) - start[e_s])
    n_blocks = (A + N_EXPERTS * (MOE_BLOCK - 1) + MOE_BLOCK - 1) // MOE_BLOCK
    P = n_blocks * MOE_BLOCK
    tok_buf = jnp.zeros((P,), jnp.int32).at[dest].set(tok_s)
    gate_buf = jnp.zeros((P,), jnp.float32).at[dest].set(g_s)
    blk_expert = jnp.minimum(
        jnp.searchsorted(p_end, jnp.arange(n_blocks, dtype=jnp.int32) * MOE_BLOCK, side='right'),
        N_EXPERTS - 1)

    def expert_block(args):
        tb, eb = args
        xb = x[tb]
        h = jax.nn.silu(xb @ w_gate[eb]) * (xb @ w_up[eb])
        return h @ w_down[eb]

    y_buf = lax.map(expert_block, (tok_buf.reshape(n_blocks, MOE_BLOCK), blk_expert))
    y = jnp.zeros((N, D), jnp.float32).at[tok_buf].add(
        y_buf.reshape(P, D).astype(jnp.float32) * gate_buf[:, None])
    return y.astype(x.dtype)

def hierarchical_moe(x, w_rg, b_rg, w_re, b_re, w_gate, w_up, w_down):
    B, T, D = x.shape
    xt = x.reshape(B * T, D)
    xf = xt.astype(jnp.float32)
    group_p = jax.nn.softmax(xf @ w_rg.astype(jnp.float32), axis=-1)
    g_sel = jnp.argmax(group_p + b_rg.astype(jnp.float32), axis=-1)
    g_w = jnp.take_along_axis(group_p, g_sel[:, None], axis=-1)
    e_logits = (xf @ w_re.astype(jnp.float32)).reshape(B * T, N_GROUPS, EXPERTS_PER_GROUP)
    e_logits = jnp.take_along_axis(e_logits, g_sel[:, None, None], axis=1)[:, 0]
    e_p = jax.nn.softmax(e_logits, axis=-1)
    _, e_loc = lax.top_k(e_p + b_re.astype(jnp.float32)[g_sel], TOP_K_IN_GROUP)
    e_w = jnp.take_along_axis(e_p, e_loc, axis=-1)
    e_w = e_w / jnp.sum(e_w, axis=-1, keepdims=True)
    expert_ids = (g_sel[:, None] * EXPERTS_PER_GROUP + e_loc).astype(jnp.int32)
    y = routed_expert_mlps(xt, expert_ids, g_w * e_w, w_gate, w_up, w_down)
    return y.reshape(B, T, D)

def setup_inputs(seed: int = 0) -> dict:
    key = jax.random.key(seed)
    ks = jax.random.split(key, 24)
    f32 = jnp.float32
    w_buf = min(WINDOW, PAST_LEN)

    def nrm(k, shape, s):
        return jax.random.normal(k, shape, f32) * s

    dt = jnp.exp(jax.random.uniform(ks[10], (DEPTH, GDN_HEADS), f32, np.log(1e-3), np.log(1e-1)))
    return {
        'x_prompt': nrm(ks[0], (BATCH, SEQ, D_MODEL), 1.0),
        'x_sample': nrm(ks[1], (DEC_BATCH, DEC_SEQ, D_MODEL), 1.0),
        'cache_swa_k': nrm(ks[2], (DEPTH, DEC_BATCH, w_buf, SWA_KV_HEADS, HEAD_DIM), 1.0),
        'cache_swa_v': nrm(ks[3], (DEPTH, DEC_BATCH, w_buf, SWA_KV_HEADS, HEAD_DIM), 1.0),
        'state_gdn_conv': nrm(ks[4], (DEPTH, DEC_BATCH, CONV_W - 1, GDN_CONV_CH), 1.0),
        'state_gdn': nrm(ks[5], (DEPTH, DEC_BATCH, GDN_HEADS, GDN_DK, GDN_DV), 0.1),
        'norm_mix': 1.0 + nrm(ks[6], (DEPTH, D_MODEL), 0.02),
        'w_in': nrm(ks[7], (DEPTH, D_MODEL, D_IN), D_MODEL ** -0.5),
        'swa_sinks': nrm(ks[8], (DEPTH, SWA_HEADS), 0.5),
        'gdn_conv_w': nrm(ks[9], (DEPTH, CONV_W, GDN_CONV_CH), 0.5),
        'gdn_A_log': jnp.log(jax.random.uniform(ks[11], (DEPTH, GDN_HEADS), f32, 1.0, 16.0)),
        'gdn_dt_bias': dt + jnp.log(-jnp.expm1(-dt)),
        'gdn_norm_w': 1.0 + nrm(ks[12], (DEPTH, GDN_DV), 0.02),
        'w_out': nrm(ks[13], (DEPTH, D_MIX, D_MODEL), D_MIX ** -0.5),
        'norm_ffn': 1.0 + nrm(ks[14], (DEPTH, D_MODEL), 0.02),
        'w_router_group': nrm(ks[15], (DEPTH, D_MODEL, N_GROUPS), D_MODEL ** -0.5),
        'b_router_group': nrm(ks[16], (DEPTH, N_GROUPS), 0.01),
        'w_router_expert': nrm(ks[17], (DEPTH, D_MODEL, N_EXPERTS), D_MODEL ** -0.5),
        'b_router_expert': nrm(ks[18], (DEPTH, N_GROUPS, EXPERTS_PER_GROUP), 0.01),
        'w_exp_gate': nrm(ks[19], (DEPTH, N_EXPERTS, D_MODEL, D_EXPERT), D_MODEL ** -0.5),
        'w_exp_up': nrm(ks[20], (DEPTH, N_EXPERTS, D_MODEL, D_EXPERT), D_MODEL ** -0.5),
        'w_exp_down': nrm(ks[21], (DEPTH, N_EXPERTS, D_EXPERT, D_MODEL), D_EXPERT ** -0.5),
        'norm_final': 1.0 + nrm(ks[22], (D_MODEL,), 0.02),
    }

def reference(x_prompt, x_sample, cache_swa_k, cache_swa_v, state_gdn_conv, state_gdn,
              norm_mix, w_in, swa_sinks, gdn_conv_w, gdn_A_log, gdn_dt_bias, gdn_norm_w, w_out,
              norm_ffn, w_router_group, b_router_group, w_router_expert, b_router_expert,
              w_exp_gate, w_exp_up, w_exp_down, norm_final):
    hp, hs = x_prompt, x_sample
    Bp = x_prompt.shape[0]
    kp_l, vp_l, ks_l, vs_l, cp_l, cs_l, sp_l, ss_l = [], [], [], [], [], [], [], []
    for l in range(DEPTH):
        u_p = rmsnorm(hp, norm_mix[l]) @ w_in[l]
        u_s = rmsnorm(hs, norm_mix[l]) @ w_in[l]
        q_p, k_p, v_p, c_p, z_p, a_p, b_p = jnp.split(u_p, IN_SPLITS, axis=-1)
        q_s, k_s, v_s, c_s, z_s, a_s, b_s = jnp.split(u_s, IN_SPLITS, axis=-1)

        o_swa_p = swa_prompt(q_p, k_p, v_p, swa_sinks[l])
        kp_l.append(k_p.reshape(Bp, -1, SWA_KV_HEADS, HEAD_DIM)[:, -WINDOW:])
        vp_l.append(v_p.reshape(Bp, -1, SWA_KV_HEADS, HEAD_DIM)[:, -WINDOW:])
        o_swa_s, kbuf_s, vbuf_s = swa_sample(q_s, k_s, v_s, cache_swa_k[l], cache_swa_v[l], swa_sinks[l])
        ks_l.append(kbuf_s)
        vs_l.append(vbuf_s)

        ext_p = jnp.concatenate([jnp.zeros((Bp, CONV_W - 1, GDN_CONV_CH), c_p.dtype), c_p], axis=1)
        ext_s = jnp.concatenate([state_gdn_conv[l].astype(c_s.dtype), c_s], axis=1)
        cp_l.append(ext_p[:, -(CONV_W - 1):])
        cs_l.append(ext_s[:, -(CONV_W - 1):])
        S0_p = jnp.zeros((Bp, GDN_HEADS, GDN_DK, GDN_DV), jnp.float32)
        o_gdn_p, S_p = gated_deltanet(causal_short_conv(ext_p, gdn_conv_w[l]), z_p, a_p, b_p, S0_p,
                                      gdn_A_log[l], gdn_dt_bias[l], gdn_norm_w[l])
        o_gdn_s, S_s = gated_deltanet(causal_short_conv(ext_s, gdn_conv_w[l]), z_s, a_s, b_s, state_gdn[l],
                                      gdn_A_log[l], gdn_dt_bias[l], gdn_norm_w[l])
        sp_l.append(S_p.astype(state_gdn.dtype))
        ss_l.append(S_s.astype(state_gdn.dtype))

        hp = hp + jnp.concatenate([o_swa_p, o_gdn_p], axis=-1) @ w_out[l]
        hs = hs + jnp.concatenate([o_swa_s, o_gdn_s], axis=-1) @ w_out[l]

        hp = hp + hierarchical_moe(rmsnorm(hp, norm_ffn[l]), w_router_group[l], b_router_group[l],
                                   w_router_expert[l], b_router_expert[l],
                                   w_exp_gate[l], w_exp_up[l], w_exp_down[l])
        hs = hs + hierarchical_moe(rmsnorm(hs, norm_ffn[l]), w_router_group[l], b_router_group[l],
                                   w_router_expert[l], b_router_expert[l],
                                   w_exp_gate[l], w_exp_up[l], w_exp_down[l])

    y_prompt = rmsnorm(hp, norm_final)
    y_sample = rmsnorm(hs, norm_final)
    new_swa_k_prompt = jnp.stack(kp_l, axis=0)
    new_swa_v_prompt = jnp.stack(vp_l, axis=0)
    new_swa_k_sample = jnp.stack(ks_l, axis=0)
    new_swa_v_sample = jnp.stack(vs_l, axis=0)
    new_conv_prompt = jnp.stack(cp_l, axis=0)
    new_conv_sample = jnp.stack(cs_l, axis=0)
    new_gdn_prompt = jnp.stack(sp_l, axis=0)
    new_gdn_sample = jnp.stack(ss_l, axis=0)
    return (y_prompt, y_sample, new_swa_k_prompt, new_swa_v_prompt, new_swa_k_sample, new_swa_v_sample,
            new_conv_prompt, new_conv_sample, new_gdn_prompt, new_gdn_sample)


_drawn_inputs = setup_inputs


def setup_inputs(seed=0):
    import zlib

    import numpy as np

    out = dict(_drawn_inputs(seed))
    spreads = {}
    factors = {'swa_sinks': 8.0, 'norm_ffn': 2.826, 'norm_final': 2.824}
    for name, (base, spread) in spreads.items():
        noise = np.random.default_rng([zlib.crc32(name.encode()), seed]).standard_normal(out[name].shape)
        drawn = base * np.exp(spread * noise) if base else spread * noise
        out[name] = jnp.asarray(drawn.astype(out[name].dtype))
    for name, factor in factors.items():
        out[name] = (out[name] * factor).astype(out[name].dtype)
    return out
```

```python
from contextlib import ExitStack

import numpy as np
import concourse.bass as bass
from concourse import mybir

F32 = mybir.dt.float32
I32 = mybir.dt.int32
U32 = mybir.dt.uint32
ALU = mybir.AluOpType
ACT = mybir.ActivationFunctionType
AX = mybir.AxisListType.X

P = 128
D = 1024
SEQ = 2048
NT = SEQ // P
DB, DT = 8, 8
NS = DB * DT
NTOK = SEQ + NS
TILES = NT + 1
H = 8
HD = 64
KVH = 2
W = 128
CW = 4
CC = 3 * H * HD
QKV = H * HD + 2 * KVH * HD
ZAB = H * HD + 2 * H
DIN = QKV + CC + ZAB
KC = D // P
NG, EPG = 8, 8
NE = NG * EPG
NR = NG + NE
DE = D // 4
EPS = 1e-6
ATT = HD ** -0.5
LEVELS = [2, 4, 8, 16, 32, 64]
SLEVELS = [2, 4]
MAXB = (2 * NTOK + NE * (P - 1)) // P + 1
MINB = 2 * NTOK // P
ZFILL = -(-(MAXB + 2 - MINB) // (NT // 2 - 1))
SLOT_BLOCKS = MAXB + 4
NEG = -1e30


def constants():
    i = np.arange(P)
    c = {}
    c["ident"] = np.eye(P)
    c["upto"] = (i[:, None] <= i[None, :])
    c["after"] = (i[:, None] > i[None, :])
    c["strict"] = (i[:, None] < i[None, :])
    c["pair1"] = (i[:, None] // 2 == i[None, :] // 2) & (i[:, None] < i[None, :])
    same = (i[:, None] // DT == i[None, :] // DT)
    c["s_upto"] = c["upto"] & same
    c["s_after"] = c["after"] & same
    c["s_strict"] = c["strict"] & same
    c["ones"] = np.ones((P, P))
    c["s_same"] = same
    lv = np.zeros((P, len(LEVELS), P // 2))
    for n, s in enumerate(LEVELS):
        e = np.arange(P // 2)
        j = e // s * 2 * s + e % s
        lv[:, n] = (i[:, None] // s == j[None, :] // s + 1)
    c["levels"] = lv.reshape(P, -1)
    k = np.arange(2 * W)
    qi = W + i
    band = (k[None, :] <= qi[:, None]) & (qi[:, None] - k[None, :] < W)
    c["band"] = np.where(band, 0.0, NEG)
    c["band0"] = np.where(band & (k[None, :] >= W), 0.0, NEG)
    ks = np.arange(W + DT)
    qs = W + i % DT
    c["s_band"] = np.where((ks[None, :] <= qs[:, None]) & (qs[:, None] - ks[None, :] < W), 0.0, NEG)
    c["s_own"] = (i[:, None] // DT == np.arange(DB)[None, :])
    c["qscale"] = np.tile(np.where(np.arange(2 * H) < H, HD ** -0.5, 1.0), (P, 1))
    c["first8"] = np.tile(NG - np.arange(NG), (P, 1))
    c["half"] = np.full((P, 2 * H), -0.5)
    c["tokid"] = (np.arange(TILES)[None, :] * P + i[:, None])
    c["blockid"] = np.tile(np.arange(MAXB + 1), (P, 1))
    c["block128"] = np.tile(np.arange(NTOK // P + 1) * P, (P, 1))
    return {k: np.ascontiguousarray(v, dtype=np.float32) for k, v in c.items()}


CONST_SHAPES = {k: v.shape for k, v in constants().items()}


class Chain:

    def __init__(self, eng, sem):
        self.eng, self.sem, self.base, self.n = eng, sem, 0, 0

    def at(self, base):
        self.base, self.n = base, 0

    def __call__(self, ins):
        self.n += 1
        ins.then_inc(self.sem, 1)
        self.eng.wait_ge(self.sem, self.base + self.n)


class Phase(ExitStack):

    def __init__(self, nc, prefix):
        super().__init__()
        self.nc, self.prefix, self.sems = nc, prefix, []

    def sb(self, name, shape, dt=F32):
        return self.enter_context(self.nc.sbuf_tensor(self.prefix + name, shape, dt))

    def psum(self, shape, name="ps"):
        return self.enter_context(self.nc.psum_tensor(self.prefix + name, shape, F32))

    def sem(self, name):
        self.sems.append(self.enter_context(self.nc.semaphore(self.prefix + name)))
        return self.sems[-1]

    def block(self):
        self.push(lambda kind, error, trace: self.clear() if kind is None else None)
        return self.enter_context(self.nc.Block())

    def clear(self):
        with self.nc.Block() as block:
            @block.sync
            def _(sp):
                for sem in self.sems:
                    sp.sem_clear(sem)


def apart(eng, held, value):
    eng.nop(nofuse=True)
    eng.wait_ge(held, value)


def rows(ap, i, n=P):
    return ap[bass.ds(i * P, n), :]


def project_in(nc, A, S):
    GROUPS = [(g, min(512, DIN - g)) for g in range(0, DIN, 512)]
    xs = A["x_sample"].rearrange("b t d -> (b t) d")
    xp = A["x_prompt"][0]
    w_in = A["w_in"][0].rearrange("(c p) n -> c p n", p=P)
    with Phase(nc, "p1_") as ctx:
        sb, sem = ctx.sb, ctx.sem
        w = sb("w", [P, KC, DIN])
        gain = sb("gain", [P, D])
        ident = sb("ident", [P, P])
        half = sb("half", [P, 2 * H])
        x = [sb(f"x{b}", [P, D]) for b in range(2)]
        sq = sb("sq", [P, D])
        ss = [sb(f"ss{b}", [P, 1]) for b in range(2)]
        ms = [sb(f"ms{b}", [P, 1]) for b in range(2)]
        rstd = [sb(f"rstd{b}", [P, 1]) for b in range(2)]
        xn = [sb(f"xn{b}", [P, D]) for b in range(2)]
        xt = [sb(f"xt{b}", [P, KC, P]) for b in range(2)]
        u = [sb(f"u{b}", [P, DIN]) for b in range(2)]
        zero = sb("zero", [P, CC])
        pt = ctx.psum([P, 2, 512], "pt")
        pu = ctx.psum([P, 6, 512], "pu")

        w_in_sb = [sem(f"w{c}_loaded") for c in range(KC)]
        consts_in = sem("consts_loaded")
        x_in = [sem(f"x{b}_loaded") for b in range(2)]
        squared = sem("squared")
        pool_own = sem("pool_own")
        rstd_ready = sem("rstd_ready")
        xn_ready = sem("xn_ready")
        turned = sem("turned")
        xt_vec = sem("xt_vec")
        xt_act = sem("xt_act")
        group_done = sem("group_done")
        u_vec = sem("u_vec")
        u_act = sem("u_act")
        u_out = [sem(f"u{b}_stored") for b in range(2)]
        zeroed = sem("zeroed")
        misc_out = sem("misc_stored")
        y_cleared = sem("y_cleared")

        def n_rows(i):
            return NS if isinstance(i, int) and i == NT else P

        block = ctx.block()

        @block.sync
        def _(sp):
            def load_x(i, b):
                r = n_rows(i)
                src = xs if r == NS else rows(xp, i)
                sp.dma_start(x[b][0:r, :], src).then_inc(x_in[b], 16)

            def store_u(i, b):
                r = n_rows(i)
                sp.wait_ge(u_vec, 3 * (i + 1))
                sp.wait_ge(u_act, 3 * (i + 1))
                if r == NS:
                    conv = S["conv_s"].rearrange("(b t) n -> b t n", b=DB)[:, CW - 1:, :]
                else:
                    conv = S["conv_p"][bass.ds(i * P + CW - 1, P), :]
                sp.dma_start(conv, u[b][0:r, QKV:QKV + CC]).then_inc(u_out[b], 16)
                sp.dma_start(rows(S["qkv"], i, r), u[b][0:r, 0:QKV]).then_inc(u_out[b], 16)
                sp.dma_start(rows(S["zab"], i, r), u[b][0:r, QKV + CC:]).then_inc(u_out[b], 16)

            for b in range(2):
                sp.sem_inc(u_out[b], 16)
            load_x(0, 0)
            sp.dma_start(gain[:], A["norm_mix"].to_broadcast([P, D])).then_inc(consts_in, 16)
            sp.dma_start(ident[:], A["c_ident"]).then_inc(consts_in, 16)
            sp.dma_start(half[:], A["c_half"]).then_inc(consts_in, 16)
            for c in range(KC):
                sp.dma_start(w[:, c, :], w_in[c]).then_inc(w_in_sb[c], 16)
            load_x(1, 1)
            sp.wait_ge(zeroed, 1)
            sp.dma_start(S["conv_p"][0:CW - 1, :], zero[0:CW - 1, :]).then_inc(misc_out, 16)
            sp.dma_start(S["conv_s"].rearrange("(b t) n -> b t n", b=DB)[:, 0:CW - 1, :],
                         A["state_gdn_conv"][0]).then_inc(misc_out, 16)
            with sp.Fori(0, NT - 3, 2) as i:
                for b in range(2):
                    store_u(i + b, b)
                    sp.wait_ge(xn_ready, i + b + 1)
                    load_x(i + b + 2, b)
                sp.dma_start(S["y"][bass.ds(MINB * P + i * (ZFILL * P // 2), ZFILL * P)]
                             .rearrange("(n p) d -> p n d", p=P),
                             zero[:, 0:D].unsqueeze(1).to_broadcast([P, ZFILL, D])).then_inc(y_cleared, 16)
            store_u(NT - 2, 0)
            sp.wait_ge(xn_ready, NT - 1)
            load_x(NT, 0)
            store_u(NT - 1, 1)
            store_u(NT, 0)
            sp.wait_ge(u_out[0], 48 * (NT // 2 + 1) + 16)
            sp.wait_ge(u_out[1], 48 * (NT // 2) + 16)
            sp.wait_ge(misc_out, 32)
            sp.wait_ge(y_cleared, 16 * (NT // 2 - 1))

        @block.gpsimd
        def _(pool):
            own = Chain(pool, pool_own)
            nc.gpsimd.memset(zero[:], 0.0).then_inc(zeroed, 1)
            pool.wait_ge(consts_in, 48)

            def inverse_root(i, b):
                own.at(i)
                pool.wait_ge(squared, i + 1)
                apart(pool, consts_in, 48)
                own(nc.gpsimd.tensor_scalar(ms[b][:], ss[b][:], 1.0 / D, EPS, ALU.mult, ALU.add))
                nc.gpsimd.tensor_tensor(rstd[b][:], ms[b][:], half[:, 0:1], ALU.pow).then_inc(rstd_ready, 1)

            with pool.Fori(0, NT - 1, 2) as i:
                for b in range(2):
                    inverse_root(i + b, b)
            inverse_root(NT, 0)

        @block.scalar
        def _(act):
            def evacuate(i, b):
                act.wait_ge(turned, 2 * i + 2)
                nc.scalar.copy(xt[b][:, 4:8, :],
                               pt[:, 1, :].rearrange("p (c t) -> p c t", c=4)).then_inc(xt_act, 1)

            def groups(i, b, r):
                act.wait_ge(u_out[b], 24 * (i - b) + 16)
                for n in (0, 2, 4):
                    g, wd = GROUPS[n]
                    act.wait_ge(group_done, 6 * i + n + 1)
                    dst, src = u[b][0:r, g:g + wd], pu[0:r, n, 0:wd]
                    if n == 0:
                        dst = dst.rearrange("p (m a d) -> p a m d", m=4, a=2)
                        src = src.rearrange("p (a m d) -> p a m d", m=4, a=2)
                    nc.scalar.copy(dst, src).then_inc(u_act, 1)

            act.wait_ge(x_in[0], 16)
            nc.scalar.activation(sq[:], x[0][:], ACT.Square, accum_out=ss[0][:]).then_inc(squared, 1)
            with act.Fori(0, NT - 1, 2) as i:
                for b in range(2):
                    evacuate(i + b, b)
                    act.wait_ge(x_in[1 - b], 8 * i + 16 + 16 * b)
                    nc.scalar.activation(sq[:], x[1 - b][:], ACT.Square,
                                         accum_out=ss[1 - b][:]).then_inc(squared, 1)
                    groups(i + b, b, P)
            evacuate(NT, 0)
            groups(NT, 0, NS)

        @block.vector
        def _(dve):
            def norm(i, b):
                dve.wait_ge(rstd_ready, i + 1)
                nc.vector.scalar_tensor_tensor(xn[b][:], x[b][:], rstd[b][:], gain[:],
                                               ALU.mult, ALU.mult).then_inc(xn_ready, 1)

            def evacuate(i, b):
                dve.wait_ge(turned, 2 * i + 1)
                nc.vector.tensor_copy(xt[b][:, 0:4, :],
                                      pt[:, 0, :].rearrange("p (c t) -> p c t", c=4)).then_inc(xt_vec, 1)

            def groups(i, b, r):
                dve.wait_ge(u_out[b], 24 * (i - b) + 16)
                for n in (1, 3, 5):
                    g, wd = GROUPS[n]
                    dve.wait_ge(group_done, 6 * i + n + 1)
                    nc.vector.tensor_copy(u[b][0:r, g:g + wd], pu[0:r, n, 0:wd]).then_inc(u_vec, 1)

            dve.wait_ge(consts_in, 48)
            norm(0, 0)
            with dve.Fori(0, NT - 1, 2) as i:
                for b in range(2):
                    evacuate(i + b, b)
                    norm(i + b + 1, 1 - b)
                    groups(i + b, b, P)
            evacuate(NT, 0)
            groups(NT, 0, NS)

        @block.tensor
        def _(pe):
            pe.wait_ge(consts_in, 48)

            def tile(i, b, r, first=False):
                pe.wait_ge(xn_ready, i + 1)
                for bank in range(2):
                    if not first:
                        pe.wait_ge(xt_act if bank else xt_vec, i)
                    for c in range(4):
                        k = 4 * bank + c
                        t = nc.tensor.transpose(pt[:, bank, c * P:(c + 1) * P],
                                                xn[b][:, k * P:(k + 1) * P], ident[:])
                    t.then_inc(turned, 1)
                pe.wait_ge(xt_vec, i + 1)
                pe.wait_ge(xt_act, i + 1)
                for n, (g, wd) in enumerate(GROUPS):
                    if not first:
                        pe.wait_ge(u_vec if n % 2 else u_act, 3 * i - 2 + n // 2)
                    for c in range(KC):
                        if first:
                            pe.wait_ge(w_in_sb[c], 16)
                        m = nc.tensor.matmul(pu[0:r, n, 0:wd], xt[b][:, c, 0:r], w[:, c, g:g + wd],
                                             start=(c == 0), stop=(c == KC - 1))
                    m.then_inc(group_done, 1)

            tile(0, 0, P, first=True)
            tile(1, 1, P)
            with pe.Fori(2, NT, 2) as i:
                for b in range(2):
                    tile(i + b, b, P)
            tile(NT, 0, NS)


def token_gates(nc, A, S):
    with Phase(nc, "p2_") as ctx:
        sb, sem = ctx.sb, ctx.sem
        ab = sb("ab", [P, TILES, 2 * H])
        log_rate = sb("log_rate", [P, H])
        shift = sb("shift", [P, H])
        a = sb("a", [P, TILES, H])
        e = sb("e", [P, TILES, 2 * H])
        soft = sb("soft", [P, TILES, H])
        gb = sb("gb", [P, TILES, 2 * H])
        cleared, loaded, vec_own, act_own = sem("cleared"), sem("loaded"), sem("vec_own"), sem("act_own")
        abs_ready, exps_ready, log_ready, gb_ready, stored = (
            sem("abs_ready"), sem("exps_ready"), sem("log_ready"), sem("gb_ready"), sem("stored"))
        last = S["zab"][:, H * HD:]
        gb_rows = S["gb"].rearrange("(n p) c -> p n c", p=P)
        block = ctx.block()

        @block.sync
        def _(sp):
            sp.wait_ge(cleared, 1)
            with nc.allow_non_contiguous_dma(reason="16 gate columns of each row"):
                sp.dma_start(ab[:, 0:NT, :], last[0:SEQ].rearrange("(n p) c -> p n c", p=P)).then_inc(loaded, 16)
                sp.dma_start(ab[0:NS, NT, :], last[SEQ:NTOK]).then_inc(loaded, 16)
            sp.dma_start(log_rate[:], A["gdn_A_log"].to_broadcast([P, H])).then_inc(loaded, 16)
            sp.dma_start(shift[:], A["gdn_dt_bias"].to_broadcast([P, H])).then_inc(loaded, 16)
            sp.wait_ge(gb_ready, 1)
            sp.dma_start(gb_rows, gb[:]).then_inc(stored, 16)
            sp.wait_ge(stored, 16)

        @block.vector
        def _(dve):
            own = Chain(dve, vec_own)
            nc.vector.memset(ab[:], 0.0).then_inc(cleared, 1)
            dve.wait_ge(loaded, 64)
            own(nc.vector.tensor_tensor(a[:], ab[:, :, 0:H],
                                        shift[:].unsqueeze(1).to_broadcast([P, TILES, H]), ALU.add))
            nc.vector.scalar_tensor_tensor(e[:, :, 0:H], a[:], -1.0, a[:], ALU.mult, ALU.max).then_inc(abs_ready, 1)
            dve.wait_ge(exps_ready, 1)
            own(nc.vector.tensor_scalar_add(e[:, :, H:], e[:, :, H:], 1.0))
            own(nc.vector.reciprocal(gb[:, :, H:], e[:, :, H:]))
            dve.wait_ge(log_ready, 1)
            own(nc.vector.scalar_tensor_tensor(soft[:], a[:], 0.0, soft[:], ALU.max, ALU.add))
            nc.vector.scalar_tensor_tensor(gb[:, :, 0:H], soft[:], -1.0,
                                           log_rate[:].unsqueeze(1).to_broadcast([P, TILES, H]),
                                           ALU.mult, ALU.mult).then_inc(gb_ready, 1)

        @block.scalar
        def _(act):
            own = Chain(act, act_own)
            act.wait_ge(loaded, 64)
            nc.scalar.activation(e[:, :, H:], ab[:, :, H:], ACT.Exp, scale=-1.0).then_inc(exps_ready, 1)
            own(nc.scalar.activation(log_rate[:], log_rate[:], ACT.Exp))
            act.wait_ge(abs_ready, 1)
            own(nc.scalar.activation(e[:, :, 0:H], e[:, :, 0:H], ACT.Exp, scale=-1.0))
            nc.scalar.activation(soft[:], e[:, :, 0:H], ACT.Ln, bias=1.0).then_inc(log_ready, 1)


class Signal:

    def __init__(self, sem, n, ahead=1):
        self.sem, self.n, self.ahead = sem, n, ahead

    def back(self, i, d):
        return self.n * (i + (1 + self.ahead - d))

    def before(self, i):
        return self.back(i, 1)

    def part(self, i, k):
        return self.back(i, 1) + k

    def all(self, i):
        return self.back(i, 0)


def bc(ap, shape, axis):
    return ap.unsqueeze(axis).to_broadcast(shape)


def mix_prompt(nc, A, S, O):
    GH = H * HD
    with Phase(nc, "p3_") as ctx:
        sb, sem = ctx.sb, ctx.sem
        signals = []

        def signal(name, n=1):
            signals.append(Signal(sem(name), n))
            return signals[-1]

        w_out = sb("w_out", [P, KC, D])
        w_conv = sb("w_conv", [P, CW, CC])
        w_route = sb("w_route", [P, KC, NR])
        gain = sb("gain", [P, D])
        gain_o = sb("gain_o", [P, H, HD])
        sinks = sb("sinks", [P, H])
        ident, upto, after, strict, pair1, ones = (sb(n, [P, P]) for n in
                                                   ("ident", "upto", "after", "strict", "pair1", "ones"))
        levels = sb("levels", [P, len(LEVELS), P // 2])
        band, band_now = sb("band", [P, 2 * W]), sb("band_now", [P, 2 * W])
        qscale, half = sb("qscale", [P, 2 * H]), sb("half", [P, 2 * H])
        taps = sb("taps", [P, CW, CC])
        qkv = sb("qkv", [P, QKV])
        zab = sb("zab", [P, ZAB])
        gb = sb("gb", [P, 2 * H])
        x = sb("x", [P, D])
        y = sb("y", [P, CC])
        th = sb("th", [P, CC])
        ss16, ms16, r16 = sb("ss16", [P, 2 * H]), sb("ms16", [P, 2 * H]), sb("r16", [P, 2 * H])
        gt = sb("gt", [P, H, P])
        dec, dec_s = sb("dec", [P, H, P]), sb("dec_s", [P, H, P])
        e24 = sb("e24", [P, 3 * H])
        gtot = sb("gtot", [P, H // 2])
        be = sb("be", [P, H])
        kb, kd, vb = sb("kb", [P, H, HD]), sb("kd", [P, H, HD]), sb("vb", [P, H, HD])
        kt = sb("kt", [P, H // 2, P])
        kbq = sb("kbq", [P, H // 2, 2, P])
        lt, qkt = sb("lt", [P, H, P]), sb("qkt", [P, H, P])
        inv, invt = sb("inv", [P, H, P]), sb("invt", [P, H, P])
        yc = sb("yc", [P, 2, 4, P // 2])
        r = sb("r", [P, H, HD])
        vn = sb("vn", [P, H, HD])
        o = sb("o", [P, H, HD])
        thz, zs = sb("thz", [P, H, HD]), sb("zs", [P, H, HD])
        ss8, ms8, r8 = sb("ss8", [P, H]), sb("ms8", [P, H]), sb("r8", [P, H])
        state = sb("state", [P, H // 2, HD])
        aq = sb("aq", [P, 4, P])
        ak = sb("ak", [P, 2, P])
        av = sb("av", [P, 2, KVH * HD])
        s = sb("s", [P, H, 2 * W])
        pt = sb("pt", [P, H, 2, P])
        m8, nm8, sm8, sum8, den8 = (sb(n, [P, H]) for n in ("m8", "nm8", "sm8", "sum8", "den8"))
        mix = sb("mix", [P, D])
        mixt = sb("mixt", [P, KC, P])
        h = sb("h", [P, D])
        hss, hms, hr = sb("hss", [P, 1]), sb("hms", [P, 1]), sb("hr", [P, 1])
        hn = sb("hn", [P, KC, P])
        hnt = mixt
        lg = sb("lg", [P, NR])
        ps = ctx.psum([P, 8, 512], "ps")

        consts_in = sem("consts_in")
        cleared = sem("cleared")
        stored_state = sem("stored_state")
        taps_in, qkv_in, zab_in, gb_in, x_in = (signal(n, k) for n, k in (
            ("taps_in", 64), ("qkv_in", 16), ("zab_in", 16), ("gb_in", 16), ("x_in", 16)))
        conv_ready, masked, nmax_ready, y_ready, ss_ready = (signal(n) for n in (
            "conv_ready", "masked", "nmax_ready", "y_ready", "ss_ready"))
        qk_ready, kb_ready, zs_half, swa_mixed, lt_ready, invt0_ready = (signal(n) for n in (
            "qk_ready", "kb_ready", "zs_half", "swa_mixed", "lt_ready", "invt0_ready"))
        yc_ready, inv_ready = signal("yc_ready", 2 * len(LEVELS)), signal("inv_ready", 2 * len(LEVELS))
        r_ready, qs_read, o_ready, state_ready, oss_ready, mix_ready = (signal(n) for n in (
            "r_ready", "qs_read", "o_ready", "state_ready", "oss_ready", "mix_ready"))
        h_ready, hn_ready = signal("h_ready"), signal("hn_ready")
        vec_out = signal("vec_out", 4)
        aq_ready, th_ready, thz_ready, e24_ready, gtot_ready, dec_ready, sq_ready, p_ready = (signal(n) for n in (
            "aq_ready", "th_ready", "thz_ready", "e24_ready", "gtot_ready", "dec_ready", "sq_ready", "p_ready"))
        kbq_ready = signal("kbq_ready", 3)
        pt_act = signal("pt_act")
        inv0_ready, invt_ready = signal("inv0_ready", 2), signal("invt_ready", 2 * len(LEVELS))
        vn_ready, osq_ready, mixt_act, hsq_ready, hnt_act, lg_ready = (signal(n) for n in (
            "vn_ready", "osq_ready", "mixt_act", "hsq_ready", "hnt_act", "lg_ready"))
        gt_ready, prod_ready, av_ready, decs_ready = signal("gt_ready"), signal("prod_ready", CW), signal(
            "av_ready"), signal("decs_ready")
        r16_ready, kd_ready, zs_ready, r8_ready, hr_ready, band_ready = (signal(n) for n in (
            "r16_ready", "kd_ready", "zs_ready", "r8_ready", "hr_ready", "band_ready"))
        aq_turned, scored, gates_done, dsum_done, pt_turned, pv_done, kkqk_done, inv0_turned = (
            signal(n, k) for n, k in (("aq_turned", 2), ("scored", 1), ("gates_done", 1), ("dsum_done", 1),
                                      ("pt_turned", 4), ("pv_done", 1), ("kkqk_done", 1), ("inv0_turned", 2)))
        kbq_turned = signal("kbq_turned", 3)
        yc_done, x_done, invt_turned = (signal(n, 2 * len(LEVELS)) for n in ("yc_done", "x_done", "invt_turned"))
        qs_done, v_done, o_done, kdv_done, mixt_turned, proj_done, hnt_turned, lg_done = (
            signal(n, k) for n, k in (("qs_done", 1), ("v_done", 1), ("o_done", 1), ("kdv_done", 1),
                                      ("mixt_turned", 2), ("proj_done", 2), ("hnt_turned", 2), ("lg_done", 1)))
        h_out, hn_out, lg_out = (signal(n, 16) for n in ("h_out", "hn_out", "lg_out"))
        vec_own, pool_own, act_own = signal("vec_own", VEC_OWN), signal("pool_own", POOL_OWN), signal("act_own", ACT_OWN)

        CONSTS = [(w_out, A["w_out"][0].rearrange("(c p) n -> p c n", p=P)),
                  (w_conv, A["gdn_conv_w"].to_broadcast([P, CW, CC])),
                  (w_route[:, :, 0:NG], A["w_router_group"][0].rearrange("(p c) n -> p c n", p=P)),
                  (w_route[:, :, NG:], A["w_router_expert"][0].rearrange("(p c) n -> p c n", p=P)),
                  (gain, A["norm_ffn"].to_broadcast([P, D])),
                  (gain_o, A["gdn_norm_w"].unsqueeze(1).to_broadcast([P, H, HD])),
                  (sinks, A["swa_sinks"].to_broadcast([P, H])),
                  (ident, A["c_ident"]), (upto, A["c_upto"]), (after, A["c_after"]), (strict, A["c_strict"]),
                  (pair1, A["c_pair1"]), (ones, A["c_ones"]),
                  (levels, A["c_levels"].rearrange("p (l e) -> p l e", l=len(LEVELS))),
                  (band, A["c_band"]), (band_now, A["c_band0"]), (qscale, A["c_qscale"]), (half, A["c_half"])]
        ALL_IN = 16 * len(CONSTS)
        block = ctx.block()

        @block.sync
        def _(sp):
            for sig in signals:
                sp.sem_inc(sig.sem, sig.n)
            for dst, src in CONSTS[::-1]:
                sp.dma_start(dst if isinstance(dst, bass.AP) else dst[:], src).then_inc(consts_in, 16)
            with sp.Fori(0, NT, 1) as i:
                sp.wait_ge(conv_ready.sem, conv_ready.before(i))
                for t in range(CW):
                    sp.dma_start(taps[:, t, :], S["conv_p"][bass.ds(i * P + t, P), :]).then_inc(taps_in.sem, 16)
                sp.wait_ge(aq_turned.sem, aq_turned.before(i))
                sp.wait_ge(av_ready.sem, av_ready.before(i))
                sp.dma_start(qkv[:], rows(S["qkv"], i)).then_inc(qkv_in.sem, 16)
                sp.wait_ge(kd_ready.sem, kd_ready.before(i))
                sp.wait_ge(r_ready.sem, r_ready.before(i))
                sp.wait_ge(gates_done.sem, gates_done.before(i))
                sp.dma_start(gb[:], rows(S["gb"], i)).then_inc(gb_in.sem, 16)
                sp.wait_ge(zs_half.sem, zs_half.before(i))
                sp.dma_start(zab[:], rows(S["zab"], i)).then_inc(zab_in.sem, 16)
                sp.wait_ge(h_ready.sem, h_ready.before(i))
                sp.dma_start(x[:], rows(A["x_prompt"][0], i)).then_inc(x_in.sem, 16)
            sp.wait_ge(state_ready.sem, state_ready.all(NT - 1))
            for par in range(2):
                sp.dma_start(O["gdn_prompt"][0, 0].rearrange("(m a) k v -> a k m v", a=2)[par],
                             state[par * HD:(par + 1) * HD]).then_inc(stored_state, 16)
            sp.wait_ge(stored_state, 32)
            for sig in (h_out, hn_out, lg_out):
                sp.wait_ge(sig.sem, sig.all(NT - 1))

        @block.gpsimd
        def _(pool):
            own = Chain(pool, pool_own.sem)
            nc.gpsimd.memset(av[:], 0.0)
            nc.gpsimd.memset(ak[:], 0.0)
            nc.gpsimd.memset(state[:], 0.0).then_inc(cleared, 1)
            pool.wait_ge(cleared, 1)
            pool.wait_ge(consts_in, ALL_IN)
            with pool.Fori(0, NT, 1) as i:
                own.at(pool_own.before(i))
                pool.wait_ge(gb_in.sem, gb_in.all(i))
                pool.wait_ge(dsum_done.sem, dsum_done.before(i))
                nc.gpsimd.tensor_tensor(gt[:], bc(gb[:, 0:H], [P, H, P], 2), bc(upto[:], [P, H, P], 1),
                                        ALU.mult).then_inc(gt_ready.sem, 1)
                for t in range(CW):
                    pool.wait_ge(taps_in.sem, taps_in.all(i))
                    nc.gpsimd.tensor_tensor(taps[:, t, :], taps[:, t, :], w_conv[:, t, :],
                                            ALU.mult).then_inc(prod_ready.sem, 1)
                pool.wait_ge(pv_done.sem, pv_done.before(i))
                apart(pool, consts_in, ALL_IN)
                own(nc.gpsimd.tensor_copy(av[:, 0, :], av[:, 1, :]))
                pool.wait_ge(qkv_in.sem, qkv_in.all(i))
                apart(pool, consts_in, ALL_IN)
                nc.gpsimd.tensor_copy(av[:, 1, :], qkv[:, GH + KVH * HD:QKV]).then_inc(av_ready.sem, 1)
                pool.wait_ge(dec_ready.sem, dec_ready.all(i))
                nc.gpsimd.tensor_tensor(dec_s[:], dec[:], bc(strict[:], [P, H, P], 1), ALU.mult)
                nc.gpsimd.tensor_tensor(dec[:], dec[:], bc(upto[:], [P, H, P], 1),
                                        ALU.mult).then_inc(decs_ready.sem, 1)
                pool.wait_ge(ss_ready.sem, ss_ready.all(i))
                apart(pool, consts_in, ALL_IN)
                own(nc.gpsimd.tensor_scalar_add(ms16[:], ss16[:], 4 * EPS))
                own(nc.gpsimd.tensor_tensor(ms16[:], ms16[:], half[:], ALU.pow))
                nc.gpsimd.tensor_tensor(r16[:], ms16[:], qscale[:], ALU.mult).then_inc(r16_ready.sem, 1)
                pool.wait_ge(masked.sem, masked.all(i))
                apart(pool, consts_in, ALL_IN)
                nc.gpsimd.tensor_copy(band_now[:, 0:W], band[:, 0:W]).then_inc(band_ready.sem, 1)
                pool.wait_ge(e24_ready.sem, e24_ready.all(i))
                own(nc.gpsimd.tensor_tensor(be[:], gb[:, H:], e24[:, 0:H], ALU.mult))
                pool.wait_ge(qk_ready.sem, qk_ready.all(i))
                pool.wait_ge(kdv_done.sem, kdv_done.before(i))
                nc.gpsimd.tensor_tensor(kd[:], y[:, GH:2 * GH].rearrange("p (h d) -> p h d", h=H),
                                        bc(e24[:, H:2 * H], [P, H, HD], 2), ALU.mult).then_inc(kd_ready.sem, 1)
                pool.wait_ge(zs_half.sem, zs_half.all(i))
                own(nc.gpsimd.tensor_tensor(zs[:], zs[:], gain_o[:], ALU.mult))
                apart(pool, consts_in, ALL_IN)
                nc.gpsimd.tensor_scalar_mul(zs[:], zs[:], 0.5).then_inc(zs_ready.sem, 1)
                pool.wait_ge(oss_ready.sem, oss_ready.all(i))
                apart(pool, consts_in, ALL_IN)
                own(nc.gpsimd.tensor_scalar(ms8[:], ss8[:], 1.0 / HD, EPS, ALU.mult, ALU.add))
                nc.gpsimd.tensor_tensor(r8[:], ms8[:], half[:, 0:H], ALU.pow).then_inc(r8_ready.sem, 1)
                pool.wait_ge(hsq_ready.sem, hsq_ready.all(i))
                apart(pool, consts_in, ALL_IN)
                own(nc.gpsimd.tensor_scalar(hms[:], hss[:], 1.0 / D, EPS, ALU.mult, ALU.add))
                nc.gpsimd.tensor_tensor(hr[:], hms[:], half[:, 0:1], ALU.pow).then_inc(hr_ready.sem, 1)
            assert own.n == POOL_OWN, own.n

        @block.scalar
        def _(act):
            own = Chain(act, act_own.sem)
            act.wait_ge(consts_in, ALL_IN)
            act.wait_ge(cleared, 1)
            with act.Fori(0, NT, 1) as i:
                own.at(act_own.before(i))
                act.wait_ge(scored.sem, scored.before(i))
                own(nc.scalar.copy(ak[:, 0, :], ak[:, 1, :]))
                act.wait_ge(aq_turned.sem, aq_turned.part(i, 1))
                nc.scalar.copy(aq[:], ps[:, 0, :].rearrange("p (m t) -> p m t", m=4))
                act.wait_ge(aq_turned.sem, aq_turned.all(i))
                nc.scalar.copy(ak[:, 1, :], ps[:, 1, 0:P]).then_inc(aq_ready.sem, 1)
                act.wait_ge(gates_done.sem, gates_done.all(i))
                act.wait_ge(kd_ready.sem, kd_ready.before(i))
                act.wait_ge(o_ready.sem, o_ready.before(i))
                own(nc.scalar.activation(e24[:], ps[:, 1, 256:256 + 3 * H], ACT.Exp))
                e_tot = e24[:, 2 * H:].rearrange("p (m a) -> p a m", a=2)
                act.wait_ge(state_ready.sem, state_ready.before(i))
                nc.scalar.copy(gtot[0:HD], e_tot[0:HD, 0])
                nc.scalar.copy(gtot[HD:P], e_tot[HD:P, 1]).then_inc(e24_ready.sem, 1)
                act.wait_ge(dsum_done.sem, dsum_done.all(i))
                act.wait_ge(lt_ready.sem, lt_ready.before(i))
                nc.scalar.activation(dec[:].rearrange("p h t -> p (h t)"),
                                     ps[:, 2:4, :].rearrange("p a b -> p (a b)"), ACT.Exp).then_inc(dec_ready.sem, 1)
                act.wait_ge(conv_ready.sem, conv_ready.all(i))
                nc.scalar.activation(th[:], y[:], ACT.Tanh, scale=0.5).then_inc(th_ready.sem, 1)
                act.wait_ge(zab_in.sem, zab_in.all(i))
                act.wait_ge(zs_half.sem, zs_half.before(i))
                nc.scalar.activation(thz[:], zab[:, 0:GH].rearrange("p (h d) -> p h d", h=H), ACT.Tanh,
                                     scale=0.5).then_inc(thz_ready.sem, 1)
                act.wait_ge(y_ready.sem, y_ready.all(i))
                nc.scalar.activation(th[:, 0:2 * GH], y[:, 0:2 * GH], ACT.Square).then_inc(sq_ready.sem, 1)
                act.wait_ge(nmax_ready.sem, nmax_ready.all(i))
                for k in range(H):
                    nc.scalar.activation(s[:, k, :], s[:, k, :], ACT.Exp, bias=nm8[:, k:k + 1],
                                         accum_out=sum8[:, k:k + 1])
                nc.scalar.activation(sm8[:], sm8[:], ACT.Exp).then_inc(p_ready.sem, 1)
                act.wait_ge(kbq_turned.sem, kbq_turned.part(i, 1))
                nc.scalar.copy(kt[:], ps[:, 0, :].rearrange("p (m t) -> p m t", m=4)).then_inc(kbq_ready.sem, 1)
                for n in range(2):
                    act.wait_ge(kbq_turned.sem, kbq_turned.part(i, 2 + n))
                    nc.scalar.copy(kbq[:, :, n, :], ps[:, 1 + n, :].rearrange("p (m t) -> p m t", m=4)
                                   ).then_inc(kbq_ready.sem, 1)
                act.wait_ge(pt_turned.sem, pt_turned.part(i, 2))
                nc.scalar.copy(pt[:, 0:4].rearrange("p h a t -> p (h a t)"),
                               ps[:, 4:6, :].rearrange("p a b -> p (a b)")).then_inc(pt_act.sem, 1)
                for hf in range(2):
                    act.wait_ge(inv0_turned.sem, inv0_turned.part(i, hf + 1))
                    nc.scalar.copy(inv[:, 4 * hf:4 * hf + 4, :],
                                   ps[:, 2 + 4 * hf, :].rearrange("p (h t) -> p h t", h=4)).then_inc(inv0_ready.sem, 1)
                for n in range(len(LEVELS)):
                    for hf in range(2):
                        act.wait_ge(invt_turned.sem, invt_turned.part(i, 2 * n + hf + 1))
                        nc.scalar.copy(invt[:, 4 * hf:4 * hf + 4, :],
                                       ps[:, 2 + 4 * hf, :].rearrange("p (h t) -> p h t", h=4)
                                       ).then_inc(invt_ready.sem, 1)
                act.wait_ge(v_done.sem, v_done.all(i))
                nc.scalar.copy(vn[:], ps[:, 0, :].rearrange("p (h d) -> p h d", h=H)).then_inc(vn_ready.sem, 1)
                act.wait_ge(o_ready.sem, o_ready.all(i))
                nc.scalar.activation(r[:], o[:], ACT.Square).then_inc(osq_ready.sem, 1)
                act.wait_ge(mixt_turned.sem, mixt_turned.all(i))
                nc.scalar.copy(mixt[:, 4:8, :], ps[:, 5, :].rearrange("p (c t) -> p c t", c=4)).then_inc(mixt_act.sem, 1)
                act.wait_ge(h_ready.sem, h_ready.all(i))
                act.dma_start(rows(S["h"], i), h[:]).then_inc(h_out.sem, 16)
                nc.scalar.activation(th[:, 0:D], h[:], ACT.Square, accum_out=hss[:]).then_inc(hsq_ready.sem, 1)
                act.wait_ge(hn_ready.sem, hn_ready.all(i))
                act.dma_start(rows(S["hn"], i), hn[:].rearrange("p c q -> p (c q)")).then_inc(hn_out.sem, 16)
                act.wait_ge(hnt_turned.sem, hnt_turned.all(i))
                nc.scalar.copy(hnt[:, 4:8, :], ps[:, 1, :].rearrange("p (c t) -> p c t", c=4)).then_inc(hnt_act.sem, 1)
                act.wait_ge(lg_done.sem, lg_done.all(i))
                act.wait_ge(lg_out.sem, lg_out.before(i))
                nc.scalar.copy(lg[:], ps[:, 2, 0:NR]).then_inc(lg_ready.sem, 1)
                act.wait_ge(lg_ready.sem, lg_ready.all(i))
                act.dma_start(rows(S["logits"], i), lg[:]).then_inc(lg_out.sem, 16)
            assert own.n == ACT_OWN, own.n

        @block.vector
        def _(dve):
            own = Chain(dve, vec_own.sem)
            dve.wait_ge(consts_in, ALL_IN)
            dve.wait_ge(cleared, 1)
            yh = y[:].rearrange("p (n h d) -> p n h d", n=3, h=H)

            def odd_even(t):
                return t[:].rearrange("p (m a) d -> p a m d", a=2)

            with dve.Fori(0, NT, 1) as i:
                own.at(vec_own.before(i))
                dve.wait_ge(prod_ready.sem, prod_ready.part(i, 2))
                own(nc.vector.tensor_tensor(y[:], taps[:, 0, :], taps[:, 1, :], ALU.add))
                dve.wait_ge(prod_ready.sem, prod_ready.part(i, 3))
                own(nc.vector.tensor_tensor(y[:], y[:], taps[:, 2, :], ALU.add))
                dve.wait_ge(prod_ready.sem, prod_ready.all(i))
                nc.vector.tensor_tensor(y[:], y[:], taps[:, 3, :], ALU.add).then_inc(conv_ready.sem, 1)
                dve.wait_ge(scored.sem, scored.all(i))
                dve.wait_ge(band_ready.sem, band_ready.before(i))
                nc.vector.scalar_tensor_tensor(s[:], ps[:, 4:8, :].rearrange("p a (b k) -> p (a b) k", b=2), ATT,
                                               bc(band_now[:], [P, H, 2 * W], 1), ALU.mult, ALU.add
                                               ).then_inc(masked.sem, 1)
                dve.wait_ge(masked.sem, masked.all(i))
                own(nc.vector.tensor_reduce(m8[:], s[:], AX, ALU.max))
                own(nc.vector.tensor_tensor(m8[:], m8[:], sinks[:], ALU.max))
                nc.vector.tensor_scalar_mul(nm8[:], m8[:], -1.0)
                nc.vector.tensor_tensor(sm8[:], sinks[:], m8[:], ALU.subtract).then_inc(nmax_ready.sem, 1)
                dve.wait_ge(th_ready.sem, th_ready.all(i))
                nc.vector.scalar_tensor_tensor(y[:], th[:], 1.0, y[:], ALU.add, ALU.mult).then_inc(y_ready.sem, 1)
                dve.wait_ge(thz_ready.sem, thz_ready.all(i))
                nc.vector.scalar_tensor_tensor(zs[:], thz[:], 1.0, zab[:, 0:GH].rearrange("p (h d) -> p h d", h=H),
                                               ALU.add, ALU.mult).then_inc(zs_half.sem, 1)
                dve.wait_ge(sq_ready.sem, sq_ready.all(i))
                nc.vector.tensor_reduce(ss16[:], th[:, 0:2 * GH].rearrange("p (h d) -> p h d", d=HD), AX, ALU.add
                                        ).then_inc(ss_ready.sem, 1)
                dve.wait_ge(gb_in.sem, gb_in.all(i))
                nc.vector.scalar_tensor_tensor(vb[:], yh[:, 2], 0.5, bc(gb[:, H:], [P, H, HD], 2),
                                               ALU.mult, ALU.mult)
                dve.wait_ge(r16_ready.sem, r16_ready.all(i))
                nc.vector.tensor_tensor(y[:, 0:2 * GH].rearrange("p (h d) -> p h d", d=HD),
                                        y[:, 0:2 * GH].rearrange("p (h d) -> p h d", d=HD),
                                        bc(r16[:], [P, 2 * H, HD], 2), ALU.mult).then_inc(qk_ready.sem, 1)
                dve.wait_ge(qk_ready.sem, qk_ready.all(i))
                nc.vector.tensor_tensor(kb[:], yh[:, 1], bc(gb[:, H:], [P, H, HD], 2), ALU.mult
                                        ).then_inc(kb_ready.sem, 1)
                for n in range(2):
                    dve.wait_ge(pt_turned.sem, pt_turned.part(i, 3 + n))
                    nc.vector.tensor_copy(pt[:, 4 + 2 * n:6 + 2 * n].rearrange("p h a t -> p (h a t)"),
                                          ps[:, 6 + n, :]).then_inc(vec_out.sem, 1)
                dve.wait_ge(p_ready.sem, p_ready.all(i))
                own(nc.vector.tensor_tensor(den8[:], sum8[:], sm8[:], ALU.add))
                own(nc.vector.reciprocal(den8[:], den8[:]))
                dve.wait_ge(pv_done.sem, pv_done.all(i))
                nc.vector.tensor_tensor(mix[:, 0:GH].rearrange("p (h d) -> p h d", h=H),
                                        ps[:, 3, :].rearrange("p (h d) -> p h d", h=H),
                                        bc(den8[:], [P, H, HD], 2), ALU.mult).then_inc(swa_mixed.sem, 1)
                kkqk = ps[:, 4:8, :].rearrange("p a b -> p (a b)").rearrange("p (a m c t) -> p a m c t", a=2, m=4, c=2)
                dve.wait_ge(kkqk_done.sem, kkqk_done.all(i))
                dve.wait_ge(decs_ready.sem, decs_ready.all(i))
                own(nc.vector.tensor_tensor(odd_even(lt), kkqk[:, :, :, 0, :], odd_even(dec_s), ALU.mult))
                nc.vector.tensor_tensor(odd_even(qkt), kkqk[:, :, :, 1, :], odd_even(dec), ALU.mult
                                        ).then_inc(lt_ready.sem, 1)
                own(nc.vector.tensor_tensor(invt[:], lt[:], bc(pair1[:], [P, H, P], 1), ALU.mult))
                nc.vector.tensor_tensor(invt[:], bc(ident[:], [P, H, P], 1), invt[:], ALU.subtract
                                        ).then_inc(invt0_ready.sem, 1)
                ksqs = ps[:, 0:2, :].rearrange("p a (c m d) -> p a c m d", c=2, m=4)
                dve.wait_ge(qs_done.sem, qs_done.all(i))
                dve.wait_ge(kd_ready.sem, kd_ready.all(i))
                own(nc.vector.tensor_tensor(odd_even(r), ksqs[:, :, 0],
                                            bc(be[:].rearrange("p (m a) -> p a m", a=2), [P, 2, 4, HD], 3), ALU.mult))
                nc.vector.tensor_tensor(r[:], vb[:], r[:], ALU.subtract).then_inc(r_ready.sem, 1)
                nc.vector.tensor_tensor(odd_even(o), ksqs[:, :, 1],
                                        bc(e24[:, 0:H].rearrange("p (m a) -> p a m", a=2), [P, 2, 4, HD], 3),
                                        ALU.mult).then_inc(qs_read.sem, 1)
                for n, z in enumerate(LEVELS):
                    for hf in range(2):
                        dve.wait_ge(yc_done.sem, yc_done.part(i, 2 * n + hf + 1))
                        nc.vector.tensor_tensor(yc[:, hf], ps[:, 4 * hf, 0:256].rearrange("p (h e) -> p h e", h=4),
                                                bc(levels[:, n, :], [P, 4, P // 2], 1), ALU.mult
                                                ).then_inc(yc_ready.sem, 1)
                    for hf in range(2):
                        cols = inv[:, 4 * hf:4 * hf + 4, :].rearrange("p h (b two e) -> p (h b) two e", two=2, e=z)
                        dve.wait_ge(x_done.sem, x_done.part(i, 2 * n + hf + 1))
                        nc.vector.tensor_tensor(cols[:, :, 0, :], cols[:, :, 0, :],
                                                ps[:, 1 + 4 * hf, 0:256].rearrange("p (k e) -> p k e", e=z),
                                                ALU.subtract).then_inc(inv_ready.sem, 1)
                own(nc.vector.tensor_tensor(state[:], state[:], bc(gtot[:], [P, H // 2, HD], 2), ALU.mult))
                dve.wait_ge(o_done.sem, o_done.all(i))
                nc.vector.tensor_tensor(o[:], o[:], ps[:, 1, :].rearrange("p (h d) -> p h d", h=H), ALU.add
                                        ).then_inc(o_ready.sem, 1)
                dve.wait_ge(kdv_done.sem, kdv_done.all(i))
                nc.vector.tensor_tensor(state[:], state[:], ps[:, 4, 0:256].rearrange("p (m d) -> p m d", m=4),
                                        ALU.add).then_inc(state_ready.sem, 1)
                dve.wait_ge(osq_ready.sem, osq_ready.all(i))
                nc.vector.tensor_reduce(ss8[:], r[:], AX, ALU.add).then_inc(oss_ready.sem, 1)
                dve.wait_ge(r8_ready.sem, r8_ready.all(i))
                own(nc.vector.tensor_tensor(o[:], o[:], bc(r8[:], [P, H, HD], 2), ALU.mult))
                dve.wait_ge(zs_ready.sem, zs_ready.all(i))
                nc.vector.tensor_tensor(mix[:, GH:].rearrange("p (h d) -> p h d", h=H), o[:], zs[:], ALU.mult
                                        ).then_inc(mix_ready.sem, 1)
                dve.wait_ge(mixt_turned.sem, mixt_turned.part(i, 1))
                nc.vector.tensor_copy(mixt[:, 0:4, :], ps[:, 0, :].rearrange("p (c t) -> p c t", c=4)
                                      ).then_inc(vec_out.sem, 1)
                dve.wait_ge(x_in.sem, x_in.all(i))
                dve.wait_ge(h_out.sem, h_out.before(i))
                dve.wait_ge(proj_done.sem, proj_done.all(i))
                nc.vector.tensor_tensor(h[:], ps[:, 6:8, :].rearrange("p a b -> p (a b)"), x[:], ALU.add
                                        ).then_inc(h_ready.sem, 1)
                dve.wait_ge(hr_ready.sem, hr_ready.all(i))
                dve.wait_ge(hn_out.sem, hn_out.before(i))
                nc.vector.scalar_tensor_tensor(hn[:].rearrange("p c q -> p q c"),
                                               h[:].rearrange("p (q c) -> p q c", c=KC), hr[:],
                                               gain[:].rearrange("p (q c) -> p q c", c=KC),
                                               ALU.mult, ALU.mult).then_inc(hn_ready.sem, 1)
                dve.wait_ge(hnt_turned.sem, hnt_turned.part(i, 1))
                nc.vector.tensor_copy(hnt[:, 0:4, :], ps[:, 0, :].rearrange("p (c t) -> p c t", c=4)
                                      ).then_inc(vec_out.sem, 1)
            assert own.n == VEC_OWN, own.n

        @block.tensor
        def _(pe):
            pe.wait_ge(consts_in, ALL_IN)
            pe.wait_ge(cleared, 1)
            mm, tr = nc.tensor.matmul, nc.tensor.transpose

            def part(k):
                return slice((k % 2) * HD, (k % 2) * HD + HD)

            def psum_of(bank, k, n):
                at = (k % 2 * 4 + k // 2) * n
                return ps[:, bank + at // 512, at % 512:at % 512 + n]

            with pe.Fori(0, NT, 1) as i:
                pe.wait_ge(qkv_in.sem, qkv_in.all(i))
                pe.wait_ge(vec_out.sem, vec_out.before(i))
                pe.wait_ge(hnt_act.sem, hnt_act.before(i))
                for m in range(4):
                    t = tr(ps[:, 0, m * P:(m + 1) * P], qkv[:, m * P:(m + 1) * P], ident[:])
                t.then_inc(aq_turned.sem, 1)
                tr(ps[:, 1, 0:P], qkv[:, GH:GH + KVH * HD], ident[:]).then_inc(aq_turned.sem, 1)
                pe.wait_ge(gb_in.sem, gb_in.all(i))
                pe.wait_ge(aq_ready.sem, aq_ready.all(i))
                mm(ps[:, 1, 256:256 + H], upto[:], gb[:, 0:H], start=True, stop=True)
                mm(ps[:, 1, 256 + H:256 + 2 * H], after[:], gb[:, 0:H], start=True, stop=True)
                mm(ps[:, 1, 256 + 2 * H:256 + 3 * H], ones[:], gb[:, 0:H], start=True, stop=True
                   ).then_inc(gates_done.sem, 1)
                pe.wait_ge(h_ready.sem, h_ready.before(i))
                for k in range(H):
                    hp = slice((k // 4) * HD, (k // 4) * HD + HD)
                    t = mm(ps[:, 4 + k // 2, (k % 2) * 256:(k % 2) * 256 + 256], aq[hp, k % 4, :],
                           ak[hp].rearrange("p a t -> p (a t)"), start=True, stop=True)
                t.then_inc(scored.sem, 1)
                pe.wait_ge(gt_ready.sem, gt_ready.all(i))
                pe.wait_ge(lg_ready.sem, lg_ready.before(i))
                for n in range(2):
                    t = mm(ps[:, 2 + n, :], after[:], gt[:, 4 * n:4 * n + 4, :].rearrange("p h t -> p (h t)"),
                           start=True, stop=True)
                t.then_inc(dsum_done.sem, 1)
                pe.wait_ge(qk_ready.sem, qk_ready.all(i))
                for n, src in enumerate((y[:, GH:2 * GH], kb[:].rearrange("p h d -> p (h d)"), y[:, 0:GH])):
                    if n == 1:
                        pe.wait_ge(kb_ready.sem, kb_ready.all(i))
                        pe.wait_ge(e24_ready.sem, e24_ready.all(i))
                    if n == 2:
                        pe.wait_ge(dec_ready.sem, dec_ready.all(i))
                    for m in range(4):
                        t = tr(ps[:, n, m * P:(m + 1) * P], src[:, m * P:(m + 1) * P], ident[:])
                    t.then_inc(kbq_turned.sem, 1)
                pe.wait_ge(p_ready.sem, p_ready.all(i))
                for k in range(H):
                    for a in range(2):
                        t = tr(ps[:, 4 + k // 2, (k % 2) * 256 + a * P:(k % 2) * 256 + (a + 1) * P],
                               s[:, k, a * P:(a + 1) * P], ident[:])
                    if k % 2:
                        t.then_inc(pt_turned.sem, 1)
                pe.wait_ge(pt_act.sem, pt_act.all(i))
                pe.wait_ge(vec_out.sem, vec_out.part(i, 2))
                pe.wait_ge(av_ready.sem, av_ready.all(i))
                for k in range(H):
                    for a in range(2):
                        t = mm(ps[:, 3, k * HD:(k + 1) * HD], pt[:, k, a, :],
                               av[:, a, (k // 4) * HD:(k // 4) * HD + HD], start=(a == 0), stop=(a == 1))
                t.then_inc(pv_done.sem, 1)
                pe.wait_ge(kbq_ready.sem, kbq_ready.all(i))
                for k in range(H):
                    t = mm(psum_of(4, k, 256), kt[part(k), k // 2, :],
                           kbq[part(k), k // 2].rearrange("p c t -> p (c t)"), start=True, stop=True)
                t.then_inc(kkqk_done.sem, 1)
                pe.wait_ge(state_ready.sem, state_ready.before(i))
                for k in range(H):
                    t = mm(ps[:, k % 2, k // 2 * HD:(k // 2 + 1) * HD], kt[part(k), k // 2, :],
                           state[part(k), k // 2, :], start=True, stop=True)
                for k in range(H):
                    t = mm(ps[:, k % 2, 256 + k // 2 * HD:256 + (k // 2 + 1) * HD], kbq[part(k), k // 2, 1, :],
                           state[part(k), k // 2, :], start=True, stop=True)
                t.then_inc(qs_done.sem, 1)
                pe.wait_ge(invt0_ready.sem, invt0_ready.all(i))
                for hf in range(2):
                    for k in range(4):
                        t = tr(ps[:, 2 + 4 * hf, k * P:(k + 1) * P], invt[:, 4 * hf + k, :], ident[:])
                    t.then_inc(inv0_turned.sem, 1)
                pe.wait_ge(qs_read.sem, qs_read.all(i))
                for n, z in enumerate(LEVELS):
                    for hf in range(2):
                        if n == 0:
                            pe.wait_ge(inv0_ready.sem, inv0_ready.part(i, hf + 1))
                        else:
                            pe.wait_ge(inv_ready.sem, inv_ready.part(i, 2 * n + hf - 1))
                        for k in range(4):
                            cols = inv[:, 4 * hf + k, :].rearrange("p (b two e) -> p b two e", two=2, e=z)
                            t = mm(ps[:, 4 * hf, k * 64:(k + 1) * 64], lt[:, 4 * hf + k, :], cols[:, :, 0, :],
                                   start=True, stop=True)
                        t.then_inc(yc_done.sem, 1)
                    for hf in range(2):
                        pe.wait_ge(yc_ready.sem, yc_ready.part(i, 2 * n + hf + 1))
                        if n:
                            pe.wait_ge(invt_ready.sem, invt_ready.part(i, 2 * n + hf - 1))
                        for k in range(4):
                            t = mm(ps[:, 1 + 4 * hf, k * 64:(k + 1) * 64], invt[:, 4 * hf + k, :], yc[:, hf, k, :],
                                   start=True, stop=True)
                        t.then_inc(x_done.sem, 1)
                    for hf in range(2):
                        pe.wait_ge(inv_ready.sem, inv_ready.part(i, 2 * n + hf + 1))
                        for k in range(4):
                            t = tr(ps[:, 2 + 4 * hf, k * P:(k + 1) * P], inv[:, 4 * hf + k, :], ident[:])
                        t.then_inc(invt_turned.sem, 1)
                pe.wait_ge(invt_ready.sem, invt_ready.all(i))
                for k in range(H):
                    t = mm(ps[:, 0, k * HD:(k + 1) * HD], invt[:, k, :], r[:, k, :], start=True, stop=True)
                t.then_inc(v_done.sem, 1)
                pe.wait_ge(vn_ready.sem, vn_ready.all(i))
                for k in range(H):
                    t = mm(ps[:, 1, k * HD:(k + 1) * HD], qkt[:, k, :], vn[:, k, :], start=True, stop=True)
                t.then_inc(o_done.sem, 1)
                pe.wait_ge(kd_ready.sem, kd_ready.all(i))
                for k in range(H):
                    t = mm(ps[part(k), 4, (k // 2) * HD:(k // 2 + 1) * HD], kd[:, k, :], vn[:, k, :],
                           start=True, stop=True)
                t.then_inc(kdv_done.sem, 1)
                for a in range(2):
                    if a == 1:
                        pe.wait_ge(mix_ready.sem, mix_ready.all(i))
                    for c in range(4):
                        t = tr(ps[:, 5 * a, c * P:(c + 1) * P], mix[:, (4 * a + c) * P:(4 * a + c + 1) * P], ident[:])
                    t.then_inc(mixt_turned.sem, 1)
                pe.wait_ge(vec_out.sem, vec_out.part(i, 3))
                pe.wait_ge(mixt_act.sem, mixt_act.all(i))
                for n in range(2):
                    for c in range(KC):
                        t = mm(ps[:, 6 + n, :], mixt[:, c, :], w_out[:, c, n * 512:(n + 1) * 512],
                               start=(c == 0), stop=(c == KC - 1))
                    t.then_inc(proj_done.sem, 1)
                pe.wait_ge(hn_ready.sem, hn_ready.all(i))
                for a in range(2):
                    for c in range(4):
                        t = tr(ps[:, a, c * P:(c + 1) * P], hn[:, 4 * a + c, :], ident[:])
                    t.then_inc(hnt_turned.sem, 1)
                pe.wait_ge(vec_out.sem, vec_out.all(i))
                pe.wait_ge(hnt_act.sem, hnt_act.all(i))
                for c in range(KC):
                    t = mm(ps[:, 2, 0:NR], hnt[:, c, :], w_route[:, c, :], start=(c == 0), stop=(c == KC - 1))
                t.then_inc(lg_done.sem, 1)


VEC_OWN, POOL_OWN, ACT_OWN = 11, 7, 2


class Once(dict):

    def __init__(self, phase):
        self.phase = phase

    def __missing__(self, name):
        self[name] = self.phase.sem(name)
        return self[name]


def mix_samples(nc, A, S, O):
    GH = H * HD
    R = NS
    KV = KVH * HD
    BP = DB // 2
    with Phase(nc, "p4_") as ctx:
        sb, sem = ctx.sb, ctx.sem
        on = Once(ctx)
        w_out = sb("w_out", [P, KC, D])
        w_conv = sb("w_conv", [R, CW, CC])
        w_route = sb("w_route", [P, KC, NR])
        gain = sb("gain", [R, D])
        gain_o = sb("gain_o", [R, H, HD])
        sink_rows = sb("sink_rows", [P, 1])
        ident, upto, after, strict, pair1, ones = (sb(n, [P, P]) for n in
                                                   ("ident", "upto", "after", "strict", "pair1", "ones"))
        levels = sb("levels", [P, len(LEVELS), P // 2])
        own_seq = sb("own_seq", [P, DB])
        band = sb("band", [P, W + DT])
        qscale, half = sb("qscale", [P, 2 * H]), sb("half", [P, 2 * H])
        kc, vc = sb("kc", [P, DB, KV]), sb("vc", [P, DB, KV])
        v_new = sb("v_new", [DT, DB, KV])
        kct = sb("kct", [P, DB, W + DT])
        aq = sb("aq", [P, DB, 4, DT])
        s = sb("s", [P, BP, W + DT])
        pt = sb("pt", [P, BP, P])
        pt_new = sb("pt_new", [DT, BP, P])
        m4, nm4, sm4, sum4 = (sb(n, [P, BP]) for n in ("m4", "nm4", "sm4", "sum4"))
        att = sb("att", [P, BP, HD])
        taps = sb("taps", [R, CW, CC])
        qkv, zab, gb, x = sb("qkv", [R, QKV]), sb("zab", [R, ZAB]), sb("gb", [R, 2 * H]), sb("x", [R, D])
        y, th = sb("y", [R, CC]), sb("th", [R, CC])
        ss16, r16 = sb("ss16", [R, 2 * H]), sb("r16", [R, 2 * H])
        gt, dec, dec_s = (sb(n, [R, H, R]) for n in ("gt", "dec", "dec_s"))
        g_own = sb("g_own", [R, DB, H])
        e16 = sb("e16", [R, 2 * H])
        gts = sb("gts", [P, DB, H])
        be = sb("be", [R, H])
        kb, kd, vb, r, vn, o, zs = (sb(n, [R, H, HD]) for n in ("kb", "kd", "vb", "r", "vn", "o", "zs"))
        kt, kbq = sb("kt", [P, H // 2, R]), sb("kbq", [P, H // 2, 2, R])
        lt, qkt, inv, invt = (sb(n, [R, H, R]) for n in ("lt", "qkt", "inv", "invt"))
        yc = sb("yc", [R, H, R // 2])
        tmp = sb("tmp", [R, H, DB, HD])
        ss8, r8 = sb("ss8", [R, H]), sb("r8", [R, H])
        state = sb("state", [P, H // 2, DB, HD])
        mix, h = sb("mix", [R, D]), sb("h", [R, D])
        hn = taps[:, 0, 0:D].rearrange("p (c q) -> p c q", c=KC)
        mixt = sb("mixt", [P, KC, R])
        hss, hr = sb("hss", [R, 1]), sb("hr", [R, 1])
        lg = sb("lg", [R, NR])
        ps = ctx.psum([P, 8, 512], "ps")

        CONSTS = [(taps[:, t, :], S["conv_s"].rearrange("(b t) n -> b t n", b=DB)[:, t:t + DT, :]) for t in range(CW)]
        CONSTS += [(qkv[:], rows(S["qkv"], NT, R)), (zab[:], rows(S["zab"], NT, R)), (gb[:], rows(S["gb"], NT, R)),
                   (x[:], A["x_sample"].rearrange("b t d -> (b t) d")),
                   (kc[:], A["cache_swa_k"][0].rearrange("b j h d -> j b (h d)")),
                   (vc[:], A["cache_swa_v"][0].rearrange("b j h d -> j b (h d)")),
                   (v_new[:], rows(S["qkv"], NT, R)[:, GH + KV:].rearrange("(b t) c -> t b c", b=DB)),
                   (w_conv[:], A["gdn_conv_w"].to_broadcast([R, CW, CC])),
                   (w_out[:], A["w_out"][0].rearrange("(c p) n -> p c n", p=P)),
                   (w_route[:, :, 0:NG], A["w_router_group"][0].rearrange("(p c) n -> p c n", p=P)),
                   (w_route[:, :, NG:], A["w_router_expert"][0].rearrange("(p c) n -> p c n", p=P)),
                   (gain[:], A["norm_ffn"].to_broadcast([R, D])),
                   (gain_o[:], A["gdn_norm_w"].unsqueeze(1).to_broadcast([R, H, HD])),
                   (ident[:], A["c_ident"]), (upto[:], A["c_s_upto"]), (after[:], A["c_s_after"]),
                   (strict[:], A["c_s_strict"]), (pair1[:], A["c_pair1"]), (ones[:], A["c_ones"]),
                   (levels[:], A["c_levels"].rearrange("p (l e) -> p l e", l=len(LEVELS))),
                   (own_seq[:], A["c_s_own"]), (band[:], A["c_s_band"]), (qscale[:], A["c_qscale"]),
                   (half[:], A["c_half"]), (sink_rows[:], A["sink_rows"])]
        for a in range(2):
            for m in range(H // 2):
                CONSTS.append((state[a * HD:(a + 1) * HD, m], A["state_gdn"][0, :, 2 * m + a].rearrange("b k v -> k b v")))
        ALL_IN = 16 * len(CONSTS)
        s_rows = rows(S["qkv"], NT, R).rearrange("(b t) c -> b t c", b=DB)
        COPIES = []
        for name, cache, at in (("k", A["cache_swa_k"], GH), ("v", A["cache_swa_v"], GH + KV)):
            new = O[name + "_sample"][0].rearrange("b j h d -> b j (h d)")
            COPIES += [(O[name + "_prompt"][0, 0].rearrange("j h d -> j (h d)"), S["qkv"][SEQ - W:SEQ, at:at + KV]),
                       (new[:, 0:W - DT], cache[0].rearrange("b j h d -> b j (h d)")[:, DT:]),
                       (new[:, W - DT:], s_rows[:, :, at:at + KV])]
        COPIES += [(O["conv_prompt"][0, 0], S["conv_p"][SEQ:, :]),
                   (O["conv_sample"][0], S["conv_s"].rearrange("(b t) n -> b t n", b=DB)[:, DT:, :])]
        block = ctx.block()

        @block.sync
        def _(sp):
            for dst, src in CONSTS:
                sp.dma_start(dst, src).then_inc(on["loaded"], 16)
            for dst, src in COPIES:
                sp.dma_start(dst, src).then_inc(on["copied"], 16)
            sp.wait_ge(on["att_ready"], 1)
            dst = S["swa_s"].rearrange("(n a t) (h d) -> n a h t d", a=2, t=DT, h=H)
            for n in range(BP):
                for a in range(2):
                    sp.dma_start(dst[n, a], att[a * 64:(a + 1) * 64, n, :]).then_inc(on["att_stored"], 16)
            sp.wait_ge(on["att_stored"], 16 * DB)
            sp.dma_start(mix[:, 0:GH], S["swa_s"]).then_inc(on["att_back"], 16)
            sp.wait_ge(on["state_ready"], 1)
            for a in range(2):
                for m in range(H // 2):
                    sp.dma_start(O["gdn_sample"][0, :, 2 * m + a].rearrange("b k v -> k b v"),
                                 state[a * HD:(a + 1) * HD, m]).then_inc(on["state_out"], 16)
            sp.wait_ge(on["h_ready"], 1)
            sp.dma_start(rows(S["h"], NT, R), h[:]).then_inc(on["stored"], 16)
            sp.wait_ge(on["hn_ready"], 1)
            sp.dma_start(rows(S["hn"], NT, R), hn.rearrange("p c q -> p (c q)")).then_inc(on["stored"], 16)
            sp.wait_ge(on["lg_ready"], 1)
            sp.dma_start(rows(S["logits"], NT, R), lg[:]).then_inc(on["stored"], 16)
            sp.wait_ge(on["copied"], 16 * len(COPIES))
            sp.wait_ge(on["state_out"], 16 * H)
            sp.wait_ge(on["stored"], 48)

        @block.gpsimd
        def _(pool):
            own = Chain(pool, on["pool_own"])
            pool.wait_ge(on["loaded"], ALL_IN)
            for t in range(CW):
                nc.gpsimd.tensor_tensor(taps[:, t, :], taps[:, t, :], w_conv[:, t, :], ALU.mult
                                        ).then_inc(on["prod_ready"], 1)
            nc.gpsimd.tensor_tensor(gt[:], bc(gb[:, 0:H], [R, H, R], 2), bc(upto[0:R, 0:R], [R, H, R], 1),
                                    ALU.mult).then_inc(on["gt_ready"], 1)
            nc.gpsimd.tensor_tensor(g_own[:], bc(gb[:, 0:H], [R, DB, H], 1), bc(own_seq[0:R], [R, DB, H], 2),
                                    ALU.mult).then_inc(on["g_own_ready"], 1)
            pool.wait_ge(on["dec_ready"], 1)
            nc.gpsimd.tensor_tensor(dec_s[:], dec[:], bc(strict[0:R, 0:R], [R, H, R], 1), ALU.mult)
            nc.gpsimd.tensor_tensor(dec[:], dec[:], bc(upto[0:R, 0:R], [R, H, R], 1), ALU.mult
                                    ).then_inc(on["decs_ready"], 1)
            pool.wait_ge(on["ss_ready"], 1)
            own(nc.gpsimd.tensor_scalar_add(ss16[:], ss16[:], 4 * EPS))
            own(nc.gpsimd.tensor_tensor(ss16[:], ss16[:], half[0:R], ALU.pow))
            nc.gpsimd.tensor_tensor(r16[:], ss16[:], qscale[0:R], ALU.mult).then_inc(on["r16_ready"], 1)
            pool.wait_ge(on["e16_ready"], 1)
            own(nc.gpsimd.tensor_tensor(be[:], gb[:, H:], e16[:, 0:H], ALU.mult))
            pool.wait_ge(on["qk_ready"], 1)
            nc.gpsimd.tensor_tensor(kd[:], y[:, GH:2 * GH].rearrange("p (h d) -> p h d", h=H),
                                    bc(e16[:, H:], [R, H, HD], 2), ALU.mult).then_inc(on["kd_ready"], 1)
            pool.wait_ge(on["zs_half"], 1)
            own(nc.gpsimd.tensor_tensor(zs[:], zs[:], gain_o[:], ALU.mult))
            nc.gpsimd.tensor_scalar_mul(zs[:], zs[:], 0.5).then_inc(on["zs_ready"], 1)
            pool.wait_ge(on["oss_ready"], 1)
            own(nc.gpsimd.tensor_scalar(ss8[:], ss8[:], 1.0 / HD, EPS, ALU.mult, ALU.add))
            nc.gpsimd.tensor_tensor(r8[:], ss8[:], half[0:R, 0:H], ALU.pow).then_inc(on["r8_ready"], 1)
            pool.wait_ge(on["hsq_ready"], 1)
            own(nc.gpsimd.tensor_scalar(hss[:], hss[:], 1.0 / D, EPS, ALU.mult, ALU.add))
            nc.gpsimd.tensor_tensor(hr[:], hss[:], half[0:R, 0:1], ALU.pow).then_inc(on["hr_ready"], 1)

        @block.scalar
        def _(act):
            act.wait_ge(on["keys_turned"], 3)
            nc.scalar.copy(kct[:, 0:4, 0:W], ps[:, 0, :].rearrange("p (b j) -> p b j", b=4))
            nc.scalar.copy(kct[:, 4:8, 0:W], ps[:, 1, :].rearrange("p (b j) -> p b j", b=4))
            nc.scalar.copy(kct[:, :, W:], ps[:, 2, 256:256 + R].rearrange("p (b t) -> p b t", b=DB))
            nc.scalar.copy(aq[:].rearrange("p b m t -> p m b t"),
                           ps[:, 2, 0:4 * R].rearrange("p (m b t) -> p m b t", m=4, b=DB)).then_inc(on["keys_ready"], 1)
            act.wait_ge(on["conv_ready"], 1)
            nc.scalar.activation(th[:], y[:], ACT.Tanh, scale=0.5).then_inc(on["th_ready"], 1)
            nc.scalar.activation(zs[:], zab[:, 0:GH].rearrange("p (h d) -> p h d", h=H), ACT.Tanh, scale=0.5
                                 ).then_inc(on["thz_ready"], 1)
            act.wait_ge(on["nmax_ready"], 1)
            for n in range(BP):
                nc.scalar.activation(s[:, n, :], s[:, n, :], ACT.Exp, bias=nm4[:, n:n + 1], accum_out=sum4[:, n:n + 1])
            nc.scalar.activation(sm4[:], sm4[:], ACT.Exp).then_inc(on["p_ready"], 1)
            act.wait_ge(on["gates_done"], 1)
            nc.scalar.activation(e16[:], ps[0:R, 3, 0:2 * H], ACT.Exp)
            nc.scalar.activation(gts[:].rearrange("p b h -> p (b h)"), ps[:, 3, 64:64 + DB * H], ACT.Exp
                                 ).then_inc(on["e16_ready"], 1)
            act.wait_ge(on["dsum_done"], 1)
            nc.scalar.activation(dec[:].rearrange("p h t -> p (h t)"), ps[0:R, 4, :], ACT.Exp
                                 ).then_inc(on["dec_ready"], 1)
            act.wait_ge(on["y_ready"], 1)
            nc.scalar.activation(th[:, 0:2 * GH], y[:, 0:2 * GH], ACT.Square).then_inc(on["sq_ready"], 1)
            act.wait_ge(on["pt_turned"], 1)
            nc.scalar.copy(pt[:].rearrange("p n t -> p (n t)"), ps[:, 5, :])
            nc.scalar.copy(pt_new[:].rearrange("p n t -> p (n t)"), ps[0:DT, 6, :]).then_inc(on["pt_ready"], 1)
            act.wait_ge(on["kbq_turned"], 1)
            for n in range(2):
                nc.scalar.copy(kbq[:, :, n, :], ps[:, 1 + n, 0:4 * R].rearrange("p (m t) -> p m t", m=4))
            nc.scalar.copy(kt[:], ps[:, 0, 0:4 * R].rearrange("p (m t) -> p m t", m=4)).then_inc(on["kbq_ready"], 1)
            for n in range(1 + len(SLEVELS)):
                act.wait_ge(on["inv_turned"], n + 1)
                nc.scalar.copy((invt if n else inv)[:], ps[0:R, 2, :].rearrange("p (h t) -> p h t", h=H)
                               ).then_inc(on["inv_copied"], 1)
            act.wait_ge(on["v_done"], 1)
            nc.scalar.copy(vn[:], ps[0:R, 0, :].rearrange("p (h d) -> p h d", h=H)).then_inc(on["vn_ready"], 1)
            act.wait_ge(on["o_ready"], 1)
            nc.scalar.activation(r[:], o[:], ACT.Square).then_inc(on["osq_ready"], 1)
            act.wait_ge(on["mixt_turned"], 1)
            nc.scalar.copy(mixt[:], ps[:, 4, :].rearrange("p (c t) -> p c t", c=KC)).then_inc(on["mixt_ready"], 1)
            act.wait_ge(on["h_ready"], 1)
            nc.scalar.activation(th[:, 0:D], h[:], ACT.Square, accum_out=hss[:]).then_inc(on["hsq_ready"], 1)
            act.wait_ge(on["hnt_turned"], 1)
            nc.scalar.copy(mixt[:], ps[:, 5, :].rearrange("p (c t) -> p c t", c=KC)).then_inc(on["hnt_ready"], 1)
            act.wait_ge(on["lg_done"], 1)
            nc.scalar.copy(lg[:], ps[0:R, 2, 0:NR]).then_inc(on["lg_ready"], 1)

        @block.vector
        def _(dve):
            own = Chain(dve, on["vec_own"])
            tt = nc.vector.tensor_tensor
            yh = y[:].rearrange("p (n h d) -> p n h d", n=3, h=H)

            def odd_even(t):
                return t[:].rearrange("p (m a) d -> p a m d", a=2)

            dve.wait_ge(on["loaded"], ALL_IN)
            dve.wait_ge(on["prod_ready"], 2)
            own(tt(y[:], taps[:, 0, :], taps[:, 1, :], ALU.add))
            dve.wait_ge(on["prod_ready"], 3)
            own(tt(y[:], y[:], taps[:, 2, :], ALU.add))
            dve.wait_ge(on["prod_ready"], 4)
            tt(y[:], y[:], taps[:, 3, :], ALU.add).then_inc(on["conv_ready"], 1)
            dve.wait_ge(on["scored"], 1)
            own(nc.vector.scalar_tensor_tensor(s[:, 0:2], ps[:, 5, 0:2 * (W + DT)].rearrange("p (n k) -> p n k", n=2),
                                               ATT, bc(band[:], [P, 2, W + DT], 1), ALU.mult, ALU.add))
            own(nc.vector.scalar_tensor_tensor(s[:, 2:4], ps[:, 6, 0:2 * (W + DT)].rearrange("p (n k) -> p n k", n=2),
                                               ATT, bc(band[:], [P, 2, W + DT], 1), ALU.mult, ALU.add))
            own(nc.vector.tensor_reduce(m4[:], s[:], AX, ALU.max))
            own(nc.vector.tensor_scalar(m4[:], m4[:], sink_rows[:], None, ALU.max))
            own(nc.vector.tensor_scalar_mul(nm4[:], m4[:], -1.0))
            nc.vector.tensor_scalar(sm4[:], nm4[:], sink_rows[:], None, ALU.add).then_inc(on["nmax_ready"], 1)
            dve.wait_ge(on["th_ready"], 1)
            nc.vector.scalar_tensor_tensor(y[:], th[:], 1.0, y[:], ALU.add, ALU.mult).then_inc(on["y_ready"], 1)
            dve.wait_ge(on["thz_ready"], 1)
            nc.vector.scalar_tensor_tensor(zs[:], zs[:], 1.0, zab[:, 0:GH].rearrange("p (h d) -> p h d", h=H),
                                           ALU.add, ALU.mult).then_inc(on["zs_half"], 1)
            dve.wait_ge(on["sq_ready"], 1)
            nc.vector.tensor_reduce(ss16[:], th[:, 0:2 * GH].rearrange("p (h d) -> p h d", d=HD), AX, ALU.add
                                    ).then_inc(on["ss_ready"], 1)
            dve.wait_ge(on["y_ready"], 1)
            nc.vector.scalar_tensor_tensor(vb[:], yh[:, 2], 0.5, bc(gb[:, H:], [R, H, HD], 2), ALU.mult, ALU.mult)
            dve.wait_ge(on["r16_ready"], 1)
            qk = y[:, 0:2 * GH].rearrange("p (h d) -> p h d", d=HD)
            tt(qk, qk, bc(r16[:], [R, 2 * H, HD], 2), ALU.mult).then_inc(on["qk_ready"], 1)
            dve.wait_ge(on["qk_ready"], 1)
            tt(kb[:], yh[:, 1], bc(gb[:, H:], [R, H, HD], 2), ALU.mult).then_inc(on["kb_ready"], 1)
            dve.wait_ge(on["p_ready"], 1)
            own(tt(sum4[:], sum4[:], sm4[:], ALU.add))
            own(nc.vector.reciprocal(sum4[:], sum4[:]))
            dve.wait_ge(on["pv_done"], 1)
            tt(att[:], ps[:, 7, 0:BP * HD].rearrange("p (n d) -> p n d", n=BP), bc(sum4[:], [P, BP, HD], 2), ALU.mult
               ).then_inc(on["att_ready"], 1)
            dve.wait_ge(on["kkqk_done"], 1)
            dve.wait_ge(on["decs_ready"], 1)
            kk = ps[0:R, 4:6, :].rearrange("p a (m c t) -> p a m c t", m=4, c=2)
            own(tt(odd_even(lt), kk[:, :, :, 0, :], odd_even(dec_s), ALU.mult))
            tt(odd_even(qkt), kk[:, :, :, 1, :], odd_even(dec), ALU.mult).then_inc(on["lt_ready"], 1)
            own(tt(invt[:], lt[:], bc(pair1[0:R, 0:R], [R, H, R], 1), ALU.mult))
            tt(invt[:], bc(ident[0:R, 0:R], [R, H, R], 1), invt[:], ALU.subtract).then_inc(on["invt0_ready"], 1)
            for n, z in enumerate(SLEVELS):
                dve.wait_ge(on["yc_done"], n + 1)
                tt(yc[:], ps[0:R, 0, 0:256].rearrange("p (h e) -> p h e", h=H),
                   bc(levels[0:R, n, 0:R // 2], [R, H, R // 2], 1), ALU.mult).then_inc(on["yc_ready"], 1)
                cols = inv[:].rearrange("p h (b two e) -> p (h b) two e", two=2, e=z)
                dve.wait_ge(on["x_done"], n + 1)
                tt(cols[:, :, 0, :], cols[:, :, 0, :], ps[0:R, 1, 0:256].rearrange("p (k e) -> p k e", e=z),
                   ALU.subtract).then_inc(on["inv_ready"], 1)
            for half_ in range(2):
                dve.wait_ge(on["ks_done"], half_ + 1)
                for a, dst in enumerate((r, o)):
                    for k in range(4):
                        hh = 4 * half_ + k
                        own(tt(tmp[:, hh], ps[0:R, 4 * a + k, :].rearrange("p (b d) -> p b d", b=DB),
                               bc(own_seq[0:R], [R, DB, HD], 2), ALU.mult))
                        ins = nc.vector.tensor_reduce(dst[:, hh, :], tmp[:, hh].rearrange("p b d -> p d b"), AX, ALU.add)
                        own(ins)
                dve.sem_inc(on["ks_read"], 1)
            dve.wait_ge(on["kd_ready"], 1)
            own(tt(r[:], r[:], bc(be[:], [R, H, HD], 2), ALU.mult))
            tt(r[:], vb[:], r[:], ALU.subtract).then_inc(on["r_ready"], 1)
            own(tt(o[:], o[:], bc(e16[:, 0:H], [R, H, HD], 2), ALU.mult))
            dve.wait_ge(on["vn_ready"], 1)
            tt(tmp[:], bc(vn[:], [R, H, DB, HD], 2), own_seq[0:R].unsqueeze(1).unsqueeze(3).to_broadcast([R, H, DB, HD]),
               ALU.mult).then_inc(on["vm_ready"], 1)
            dve.wait_ge(on["o_done"], 1)
            tt(o[:], o[:], ps[0:R, 1, :].rearrange("p (h d) -> p h d", h=H), ALU.add).then_inc(on["o_ready"], 1)
            g4 = gts[:].rearrange("p b (m a) -> p a m b", a=2)
            for a in range(2):
                hp = slice(a * HD, (a + 1) * HD)
                own(tt(state[hp], state[hp], bc(g4[hp, a], [HD, H // 2, DB, HD], 3), ALU.mult))
            dve.wait_ge(on["kdv_done"], 1)
            tt(state[:].rearrange("p m b d -> p m (b d)"), state[:].rearrange("p m b d -> p m (b d)"), ps[:, 4:8, :],
               ALU.add).then_inc(on["state_ready"], 1)
            dve.wait_ge(on["osq_ready"], 1)
            nc.vector.tensor_reduce(ss8[:], r[:], AX, ALU.add).then_inc(on["oss_ready"], 1)
            dve.wait_ge(on["r8_ready"], 1)
            own(tt(o[:], o[:], bc(r8[:], [R, H, HD], 2), ALU.mult))
            dve.wait_ge(on["zs_ready"], 1)
            tt(mix[:, GH:].rearrange("p (h d) -> p h d", h=H), o[:], zs[:], ALU.mult).then_inc(on["mix_ready"], 1)
            dve.wait_ge(on["proj_done"], 1)
            tt(h[:], ps[0:R, 6:8, :].rearrange("p a b -> p (a b)"), x[:], ALU.add).then_inc(on["h_ready"], 1)
            dve.wait_ge(on["h_ready"], 1)
            dve.wait_ge(on["hr_ready"], 1)
            nc.vector.scalar_tensor_tensor(hn.rearrange("p c q -> p q c"), h[:].rearrange("p (q c) -> p q c", c=KC),
                                           hr[:], gain[:].rearrange("p (q c) -> p q c", c=KC),
                                           ALU.mult, ALU.mult).then_inc(on["hn_ready"], 1)

        @block.tensor
        def _(pe):
            mm, tr = nc.tensor.matmul, nc.tensor.transpose
            pe.wait_ge(on["loaded"], ALL_IN)

            def part(k):
                return slice((k % 2) * HD, (k % 2) * HD + HD)

            for b in range(DB):
                t = tr(ps[:, b // 4, (b % 4) * P:(b % 4 + 1) * P], kc[:, b, :], ident[:])
                if b % 4 == 3:
                    t.then_inc(on["keys_turned"], 1)
            for m in range(4):
                tr(ps[:, 2, m * R:(m + 1) * R], qkv[:, m * P:(m + 1) * P], ident[0:R, 0:R])
            tr(ps[:, 2, 256:256 + R], qkv[:, GH:GH + KV], ident[0:R, 0:R]).then_inc(on["keys_turned"], 1)
            pe.wait_ge(on["g_own_ready"], 1)
            mm(ps[0:R, 3, 0:H], upto[0:R, 0:R], gb[:, 0:H], start=True, stop=True)
            mm(ps[0:R, 3, H:2 * H], after[0:R, 0:R], gb[:, 0:H], start=True, stop=True)
            mm(ps[:, 3, 64:64 + DB * H], ones[0:R, :], g_own[:].rearrange("p b h -> p (b h)"), start=True, stop=True
               ).then_inc(on["gates_done"], 1)
            mm(ps[0:R, 4, :], after[0:R, 0:R], gt[:].rearrange("p h t -> p (h t)"), start=True, stop=True
               ).then_inc(on["dsum_done"], 1)
            pe.wait_ge(on["keys_ready"], 1)
            for b in range(DB):
                for kv in range(KVH):
                    hp = slice(kv * HD, (kv + 1) * HD)
                    row, n = 64 * (b % 2) + 32 * kv, b // 2
                    t = mm(ps[row:row + 32, 5 + n // 2, (n % 2) * (W + DT):(n % 2 + 1) * (W + DT)],
                           aq[hp, b].rearrange("p m t -> p (m t)"), kct[hp, b, :], start=True, stop=True)
            t.then_inc(on["scored"], 1)
            pe.wait_ge(on["kb_ready"], 1)
            for n, src in enumerate((y[:, GH:2 * GH], kb[:].rearrange("p h d -> p (h d)"), y[:, 0:GH])):
                for m in range(4):
                    t = tr(ps[:, n, m * R:(m + 1) * R], src[:, m * P:(m + 1) * P], ident[0:R, 0:R])
            t.then_inc(on["kbq_turned"], 1)
            pe.wait_ge(on["p_ready"], 1)
            for n in range(BP):
                tr(ps[:, 5, n * P:(n + 1) * P], s[:, n, 0:W], ident[:])
                t = tr(ps[0:DT, 6, n * P:(n + 1) * P], s[:, n, W:], ident[:])
            t.then_inc(on["pt_turned"], 1)
            pe.wait_ge(on["pt_ready"], 1)
            for b in range(DB):
                for kv in range(KVH):
                    row, n = 64 * (b % 2) + 32 * kv, b // 2
                    out = ps[row:row + 32, 7, n * HD:(n + 1) * HD]
                    mm(out, pt[:, n, row:row + 32], vc[:, b, kv * HD:(kv + 1) * HD], start=True, stop=False)
                    t = mm(out, pt_new[:, n, row:row + 32], v_new[:, b, kv * HD:(kv + 1) * HD],
                           start=False, stop=True)
            t.then_inc(on["pv_done"], 1)
            pe.wait_ge(on["kbq_ready"], 1)
            pe.wait_ge(on["dec_ready"], 1)
            for k in range(H):
                t = mm(ps[0:R, 4 + k % 2, k // 2 * 2 * R:(k // 2 + 1) * 2 * R], kt[part(k), k // 2, :],
                       kbq[part(k), k // 2].rearrange("p c t -> p (c t)"), start=True, stop=True)
            t.then_inc(on["kkqk_done"], 1)
            pe.wait_ge(on["invt0_ready"], 1)
            for k in range(H):
                t = tr(ps[0:R, 2, k * R:(k + 1) * R], invt[:, k, :], ident[0:R, 0:R])
            t.then_inc(on["inv_turned"], 1)
            for n, z in enumerate(SLEVELS):
                pe.wait_ge(on["inv_copied"], n + 1)
                for k in range(H):
                    cols = inv[:, k, :].rearrange("p (b two e) -> p b two e", two=2, e=z)
                    t = mm(ps[0:R, 0, k * 32:(k + 1) * 32], lt[:, k, :], cols[:, :, 0, :], start=True, stop=True)
                t.then_inc(on["yc_done"], 1)
                pe.wait_ge(on["yc_ready"], n + 1)
                for k in range(H):
                    t = mm(ps[0:R, 1, k * 32:(k + 1) * 32], invt[:, k, :], yc[:, k, :], start=True, stop=True)
                t.then_inc(on["x_done"], 1)
                pe.wait_ge(on["inv_ready"], n + 1)
                for k in range(H):
                    t = tr(ps[0:R, 2, k * R:(k + 1) * R], inv[:, k, :], ident[0:R, 0:R])
                t.then_inc(on["inv_turned"], 1)
            pe.wait_ge(on["inv_copied"], 1 + len(SLEVELS))
            pe.wait_ge(on["att_ready"], 1)
            for half_ in range(2):
                if half_:
                    pe.wait_ge(on["ks_read"], half_)
                for a in range(2):
                    for k in range(4):
                        hh = 4 * half_ + k
                        lhs = kt[part(hh), hh // 2, :] if a == 0 else kbq[part(hh), hh // 2, 1, :]
                        t = mm(ps[0:R, 4 * a + k, :], lhs, state[part(hh), hh // 2].rearrange("p b d -> p (b d)"),
                               start=True, stop=True)
                t.then_inc(on["ks_done"], 1)
            pe.wait_ge(on["r_ready"], 1)
            pe.wait_ge(on["ks_read"], 2)
            for k in range(H):
                t = mm(ps[0:R, 0, k * HD:(k + 1) * HD], invt[:, k, :], r[:, k, :], start=True, stop=True)
            t.then_inc(on["v_done"], 1)
            pe.wait_ge(on["vn_ready"], 1)
            for k in range(H):
                t = mm(ps[0:R, 1, k * HD:(k + 1) * HD], qkt[:, k, :], vn[:, k, :], start=True, stop=True)
            t.then_inc(on["o_done"], 1)
            pe.wait_ge(on["vm_ready"], 1)
            for k in range(H):
                t = mm(ps[part(k), 4 + k // 2, :], kd[:, k, :], tmp[:, k].rearrange("p b d -> p (b d)"),
                       start=True, stop=True)
            t.then_inc(on["kdv_done"], 1)
            pe.wait_ge(on["mix_ready"], 1)
            pe.wait_ge(on["state_ready"], 1)
            pe.wait_ge(on["att_back"], 16)
            for c in range(KC):
                t = tr(ps[:, 4, c * R:(c + 1) * R], mix[:, c * P:(c + 1) * P], ident[0:R, 0:R])
            t.then_inc(on["mixt_turned"], 1)
            pe.wait_ge(on["mixt_ready"], 1)
            for n in range(2):
                for c in range(KC):
                    t = mm(ps[0:R, 6 + n, :], mixt[:, c, :], w_out[:, c, n * 512:(n + 1) * 512],
                           start=(c == 0), stop=(c == KC - 1))
            t.then_inc(on["proj_done"], 1)
            pe.wait_ge(on["hn_ready"], 1)
            for c in range(KC):
                t = tr(ps[:, 5, c * R:(c + 1) * R], hn[:, c, :], ident[0:R, 0:R])
            t.then_inc(on["hnt_turned"], 1)
            pe.wait_ge(on["hnt_ready"], 1)
            for c in range(KC):
                t = mm(ps[0:R, 2, 0:NR], mixt[:, c, :], w_route[:, c, :], start=(c == 0), stop=(c == KC - 1))
            t.then_inc(on["lg_done"], 1)


def route(nc, A, S):
    T, G, E = TILES, NG, EPG
    NB = NTOK // P + 1
    with Phase(nc, "p5_") as ctx:
        sb, sem = ctx.sb, ctx.sem
        on = Once(ctx)
        lg = sb("lg", [P, T, NR])
        b_group, b_expert = sb("b_group", [P, G]), sb("b_expert", [P, G, E])
        first8, tokid, blockid, block128 = (sb("first8", [P, G]), sb("tokid", [P, T]), sb("blockid", [1, MAXB + 1]),
                                            sb("block128", [P, NB]))
        before, ones = sb("before", [P, P]), sb("ones", [P, P])
        m = sb("m", [P, T])
        gp, ep = sb("gp", [P, T, G]), sb("ep", [P, T, E])
        cand, biased = sb("cand", [P, T, G]), sb("biased", [P, T, G])
        oh_g = sb("oh_g", [P, T, G])
        oh_e = [sb(f"oh_e{k}", [P, T, E]) for k in range(2)]
        big = sb("big", [P, T, G, E])
        oh = [sb(f"oh{k}", [P, T, G, E]) for k in range(2)]
        both = sb("both", [P, T, G, E])
        gw, ws, w = sb("gw", [P, T]), sb("ws", [P, T]), sb("w", [P, T, 2])
        base = sb("base", [P, T + 1, NE])
        nblk, blk = sb("nblk", [P, NE]), sb("blk", [P, NE, NB])
        cum = [sb(f"cum{k}", [P, NE]) for k in range(2)]
        owner, owner_of = sb("owner", [1, MAXB + 1]), sb("owner_of", [1, MAXB + 1, NE])
        dest = sb("dest", [P, T, 2])
        dest_i, tok_i, owner_i = sb("dest_i", [P, T, 2], I32), sb("tok_i", [P, T], I32), sb("owner_i", [1, MAXB + 2], I32)
        zero = sb("zero", [P, SLOT_BLOCKS], I32)
        ps = ctx.psum([P, 6, 512])

        LOADS = [(lg[:, 0:NT, :], S["logits"][0:SEQ].rearrange("(n p) c -> p n c", p=P)),
                 (lg[0:NS, NT, :], S["logits"][SEQ:NTOK]),
                 (b_group[:], A["b_router_group"].to_broadcast([P, G])),
                 (b_expert[:], A["b_router_expert"].to_broadcast([P, G, E])),
                 (first8[:], A["c_first8"]), (tokid[:], A["c_tokid"]), (blockid[:], A["c_blockid"][0:1]),
                 (block128[:], A["c_block128"]), (before[:], A["c_strict"]), (ones[:], A["c_ones"])]
        ALL_IN = 16 * len(LOADS)
        GROUPS = [(0, 512), (512, 512), (1024, T * NE - 1024)]
        block = ctx.block()

        @block.sync
        def _(sp):
            sp.wait_ge(on["cleared"], 1)
            for dst, src in LOADS:
                sp.dma_start(dst, src).then_inc(on["loaded"], 16)
            sp.dma_start(S["slots"].rearrange("(p n) o -> p (n o)", p=P), zero[:]).then_inc(on["slots_zero"], 16)
            sp.wait_ge(on["owner_ready"], 1)
            sp.dma_start(S["owner"], owner_i[:]).then_inc(on["stored"], 16)
            sp.wait_ge(on["w_ready"], 1)
            sp.dma_start(S["weights"].rearrange("(n p) k -> p n k", p=P), w[:]).then_inc(on["stored"], 16)
            sp.wait_ge(on["dest_ready"], 1)
            sp.dma_start(S["dest"].rearrange("(n p) k -> p n k", p=P), dest_i[:]).then_inc(on["stored"], 16)
            sp.wait_ge(on["stored"], 48)

        @block.gpsimd
        def _(pool):
            pool.wait_ge(on["dest_ready"], 1)
            pool.wait_ge(on["slots_zero"], 16)
            for n in range(T):
                r = P if n < NT else NS
                for k in range(2):
                    pool.indirect_dma_start(
                        out=S["slots"], out_offset=bass.IndirectOffsetOnAxis(ap=dest_i[0:r, n, k:k + 1], axis=0),
                        in_=tok_i[0:r, n:n + 1], in_offset=None).then_inc(on["scattered"], 16)
            pool.wait_ge(on["scattered"], 32 * T)

        @block.scalar
        def _(act):
            for k, t in enumerate((gp, ep)):
                act.wait_ge(on["shifted"], k + 1)
                nc.scalar.activation(t[:], t[:], ACT.Exp).then_inc(on["exps"], 1)

        @block.tensor
        def _(pe):
            pe.wait_ge(on["both_ready"], 1)
            flat = both[:].rearrange("p t g e -> p (t g e)")
            for a, lhs in enumerate((before, ones)):
                for n, (at, wd) in enumerate(GROUPS):
                    t = nc.tensor.matmul(ps[:, 3 * a + n, 0:wd], lhs[:], flat[:, at:at + wd], start=True, stop=True)
            t.then_inc(on["counted"], 1)

        @block.vector
        def _(dve):
            own = Chain(dve, on["vec_own"])
            tt, red = nc.vector.tensor_tensor, nc.vector.tensor_reduce

            def softmax_over(t, src, shape):
                own(red(m[:], src, AX, ALU.max))
                tt(t[:], src, bc(m[:], shape, 2), ALU.subtract).then_inc(on["shifted"], 1)
                dve.wait_ge(on["exps"], 1 if t is gp else 2)
                own(red(m[:], t[:], AX, ALU.add))
                own(nc.vector.reciprocal(m[:], m[:]))
                own(tt(t[:], t[:], bc(m[:], shape, 2), ALU.mult))

            def first_max(out, src, shape):
                own(red(m[:], src[:], AX, ALU.max))
                own(tt(cand[:], src[:], bc(m[:], shape, 2), ALU.is_equal))
                own(tt(cand[:], cand[:], bc(first8[:], shape, 1), ALU.mult))
                own(red(m[:], cand[:], AX, ALU.max))
                own(tt(out[:], cand[:], bc(m[:], shape, 2), ALU.is_equal))

            nc.vector.memset(zero[:], 0)
            nc.vector.memset(base[:], 0.0)
            nc.vector.memset(owner_i[:], 0)
            nc.vector.memset(lg[:], 0.0).then_inc(on["cleared"], 1)
            dve.wait_ge(on["loaded"], ALL_IN)
            s3, s4 = [P, T, G], [P, T, G, E]
            softmax_over(gp, lg[:, :, 0:G], s3)
            own(tt(biased[:], gp[:], bc(b_group[:], s3, 1), ALU.add))
            first_max(oh_g, biased, s3)
            own(tt(cand[:], gp[:], oh_g[:], ALU.mult))
            own(red(gw[:], cand[:], AX, ALU.add))
            own(tt(big[:], lg[:, :, G:].rearrange("p t (g e) -> p t g e", g=G), bc(oh_g[:], s4, 3), ALU.mult))
            own(red(biased[:], big[:].rearrange("p t g e -> p t e g"), AX, ALU.add))
            softmax_over(ep, biased[:], s3)
            own(tt(big[:], b_expert[:].unsqueeze(1).to_broadcast(s4), bc(oh_g[:], s4, 3), ALU.mult))
            own(red(biased[:], big[:].rearrange("p t g e -> p t e g"), AX, ALU.add))
            own(tt(biased[:], biased[:], ep[:], ALU.add))
            first_max(oh_e[0], biased, s3)
            own(nc.vector.scalar_tensor_tensor(biased[:], oh_e[0][:], NEG, biased[:], ALU.mult, ALU.add))
            first_max(oh_e[1], biased, s3)
            for k in range(2):
                own(tt(cand[:], ep[:], oh_e[k][:], ALU.mult))
                own(red(w[:, :, k], cand[:], AX, ALU.add))
                own(tt(oh[k][:], bc(oh_g[:], s4, 3), bc(oh_e[k][:], s4, 2), ALU.mult))
            tt(both[:], oh[0][:], oh[1][:], ALU.add).then_inc(on["both_sum"], 1)
            dve.wait_ge(on["both_sum"], 1)
            nc.vector.memset(both[NS:P, NT], 0.0).then_inc(on["both_ready"], 1)
            own(tt(ws[:], w[:, :, 0], w[:, :, 1], ALU.add))
            own(nc.vector.reciprocal(ws[:], ws[:]))
            own(tt(ws[:], ws[:], gw[:], ALU.mult))
            tt(w[:], w[:], bc(ws[:], [P, T, 2], 2), ALU.mult).then_inc(on["w_ready"], 1)
            dve.wait_ge(on["counted"], 1)
            total = ps[:, 3:6, :].rearrange("p a b -> p (a b)")
            for n in range(T):
                own(tt(base[:, n + 1, :], base[:, n, :], total[:, n * NE:(n + 1) * NE], ALU.add))
            own(tt(blk[:], bc(base[:, T, :], [P, NE, NB], 2), bc(block128[:], [P, NE, NB], 1), ALU.is_gt))
            own(red(nblk[:], blk[:], AX, ALU.add))
            own(nc.vector.tensor_copy(cum[0][:], nblk[:]))
            step, k = 1, 0
            while step < NE:
                own(nc.vector.tensor_copy(cum[1 - k][:, 0:step], cum[k][:, 0:step]))
                own(tt(cum[1 - k][:, step:], cum[k][:, step:], cum[k][:, 0:NE - step], ALU.add))
                step, k = 2 * step, 1 - k
            upto = cum[k]
            own(tt(owner_of[:], bc(blockid[:], [1, MAXB + 1, NE], 2), bc(upto[0:1], [1, MAXB + 1, NE], 1), ALU.is_ge))
            own(red(owner[:], owner_of[:], AX, ALU.add))
            own(nc.vector.tensor_scalar_min(owner[:], owner[:], float(NE - 1)))
            own(nc.vector.tensor_copy(owner_i[:, 0:MAXB + 1], owner[:]))
            nc.vector.tensor_copy(owner_i[:, MAXB + 1:], upto[0:1, NE - 1:]).then_inc(on["owner_ready"], 1)
            own(tt(nblk[:], upto[:], nblk[:], ALU.subtract))
            own(nc.vector.scalar_tensor_tensor(base[:, 0:T, :], bc(nblk[:], [P, T, NE], 1), float(P), base[:, 0:T, :],
                                               ALU.mult, ALU.add))
            own(tt(both[:].rearrange("p t g e -> p (t g e)"), base[:, 0:T, :].rearrange("p t e -> p (t e)"),
                   ps[:, 0:3, :].rearrange("p a b -> p (a b)")[:, 0:T * NE], ALU.add))
            for k in range(2):
                own(tt(oh[k][:], oh[k][:], both[:], ALU.mult))
                own(red(dest[:, :, k], oh[k][:].rearrange("p t g e -> p t (g e)"), AX, ALU.add))
            own(nc.vector.tensor_copy(tok_i[:], tokid[:]))
            nc.vector.tensor_copy(dest_i[:], dest[:]).then_inc(on["dest_ready"], 1)


def experts(nc, A, S):
    wg, wu, wd = A["w_exp_gate"][0], A["w_exp_up"][0], A["w_exp_down"][0]
    FC = DE // P
    with Phase(nc, "p6_") as ctx:
        sb, sem = ctx.sb, ctx.sem
        signals = []

        def signal(name, n=1, ahead=1):
            signals.append(Signal(sem(name), n, ahead))
            return signals[-1]

        ident = sb("ident", [P, P])
        owner = sb("owner", [1, MAXB + 2], I32)
        two = range(2)
        w_gu = [sb(f"w_gu{b}", [P, 2, KC, DE]) for b in two]
        w_dn = [sb(f"w_dn{b}", [P, FC, D]) for b in two]
        slot = [sb(f"slot{b}", [P, 1], I32) for b in two]
        x = [sb(f"x{b}", [P, D]) for b in two]
        xt = [sb(f"xt{b}", [P, KC, P]) for b in two]
        th = [sb(f"th{b}", [P, DE]) for b in two]
        mid = [sb(f"mid{b}", [P, DE]) for b in two]
        midt = [sb(f"midt{b}", [P, FC, P]) for b in two]
        y = [sb(f"y{b}", [P, D]) for b in two]
        ps = ctx.psum([P, 8, 512])

        consts_in = sem("consts_in")
        gate_in, up_in, down_in = ([signal(f"{n}{b}_in", 16) for b in two] for n in ("gate", "up", "down"))
        y_out = [signal(f"y{b}_out", 16) for b in two]
        slot_in, x_in = ([sem(f"{n}{b}_in") for b in two] for n in ("slot", "x"))
        turned, xt_vec, xt_act = (signal(n, k, 2) for n, k in (("turned", 2), ("xt_vec", 1), ("xt_act", 1)))
        gu_done, th_ready, mid_own, mid_ready = (signal(n, 1, 2) for n in ("gu_done", "th_ready", "mid_own", "mid_ready"))
        midt_turned, midt_ready, down_done = (signal(n, k, 2) for n, k in (
            ("midt_turned", 1), ("midt_ready", 1), ("down_done", 2)))
        y_vec, y_act = signal("y_vec", 1, 2), signal("y_act", 1, 2)
        block = ctx.block()

        def n_blocks(eng):
            eng.wait_ge(consts_in, 32)
            return eng.value_load(owner[0:1, MAXB + 1:MAXB + 2], min_val=1, max_val=MAXB)

        @block.sync
        def _(sp):
            for sig in signals:
                sp.sem_inc(sig.sem, sig.n * sig.ahead)
            sp.dma_start(owner[:], S["owner"]).then_inc(consts_in, 16)
            sp.dma_start(ident[:], A["c_ident"]).then_inc(consts_in, 16)
            total = n_blocks(sp)
            with sp.Fori(0, total, 2) as i:
                for b in two:
                    e = sp.value_load(owner[0:1, bass.ds(i + b, 1)], min_val=0, max_val=NE - 1)
                    sp.wait_ge(gu_done.sem, gu_done.back(i + b, 2))
                    for t, (src, sig) in enumerate(((wg, gate_in), (wu, up_in))):
                        sp.dma_start(w_gu[b][:, t].rearrange("p c f -> p (c f)"),
                                     src[bass.ds(e, 1)].rearrange("o (p c) f -> p (o c f)", p=P)).then_inc(sig[b].sem, 16)
                    sp.wait_ge(down_done.sem, down_done.back(i + b, 2))
                    sp.dma_start(w_dn[b][:].rearrange("p c f -> p (c f)"),
                                 wd[bass.ds(e, 1)].rearrange("o (p c) f -> p (o c f)", p=P)).then_inc(down_in[b].sem, 16)

        @block.gpsimd
        def _(pool):
            def gather(j, b, k):
                pool.wait_ge(turned.sem, turned.back(j, 2))
                apart(pool, consts_in, 32)
                pool.dma_start(slot[b][:], rows(S["slots"], j)).then_inc(slot_in[b], 16)
                pool.wait_ge(slot_in[b], 8 * k + 16)
                apart(pool, consts_in, 32)
                pool.indirect_dma_start(out=x[b][:], out_offset=None, in_=S["hn"],
                                        in_offset=bass.IndirectOffsetOnAxis(ap=slot[b][:, 0:1], axis=0)
                                        ).then_inc(x_in[b], 16)

            total = n_blocks(pool)
            gather(0, 0, 0)
            gather(1, 1, 0)
            with pool.Fori(0, total, 2) as i:
                for b in two:
                    gather(i + b + 2, b, i + 2)

        @block.scalar
        def _(act):
            def evacuate_x(j, b):
                act.wait_ge(turned.sem, turned.all(j))
                nc.scalar.copy(xt[b][:, 4:8, :], ps[:, 1, :].rearrange("p (c t) -> p c t", c=4)).then_inc(xt_act.sem, 1)

            total = n_blocks(act)
            evacuate_x(0, 0)
            evacuate_x(1, 1)
            with act.Fori(0, total, 2) as i:
                for b in two:
                    act.wait_ge(gu_done.sem, gu_done.all(i + b))
                    act.wait_ge(mid_ready.sem, mid_ready.back(i + b, 2))
                    nc.scalar.activation(th[b][:], ps[:, 2 + b, 0:DE], ACT.Tanh, scale=0.5).then_inc(th_ready.sem, 1)
                for b in two:
                    act.wait_ge(midt_turned.sem, midt_turned.all(i + b))
                    nc.scalar.copy(midt[b][:], ps[:, 4, 0:FC * P].rearrange("p (c t) -> p c t", c=FC)
                                   ).then_inc(midt_ready.sem, 1)
                    evacuate_x(i + b + 2, b)
                    act.wait_ge(down_done.sem, down_done.all(i + b))
                    act.wait_ge(y_out[b].sem, 8 * i + 16)
                    nc.scalar.copy(y[b][:, 512:], ps[:, 6, :]).then_inc(y_act.sem, 1)
                    act.wait_ge(y_vec.sem, y_vec.all(i + b))
                    act.wait_ge(y_act.sem, y_act.all(i + b))
                    act.dma_start(rows(S["y"], i + b), y[b][:]).then_inc(y_out[b].sem, 16)
            for b in two:
                act.wait_ge(y_out[b].sem, ((total + 1) >> 1) * 16 + 16)
            apart(act, consts_in, 32)

        @block.vector
        def _(dve):
            def evacuate_x(j, b):
                dve.wait_ge(turned.sem, turned.part(j, 1))
                nc.vector.tensor_copy(xt[b][:, 0:4, :], ps[:, 0, :].rearrange("p (c t) -> p c t", c=4)
                                      ).then_inc(xt_vec.sem, 1)

            total = n_blocks(dve)
            evacuate_x(0, 0)
            evacuate_x(1, 1)
            with dve.Fori(0, total, 2) as i:
                for b in two:
                    dve.wait_ge(th_ready.sem, th_ready.all(i + b))
                    dve.wait_ge(midt_turned.sem, midt_turned.back(i + b, 2))
                    nc.vector.scalar_tensor_tensor(mid[b][:], th[b][:], 1.0, ps[:, 2 + b, 0:DE], ALU.add, ALU.mult
                                                   ).then_inc(mid_own.sem, 1)
                    dve.wait_ge(mid_own.sem, mid_own.all(i + b))
                    nc.vector.scalar_tensor_tensor(mid[b][:], mid[b][:], 0.5, ps[:, 2 + b, DE:], ALU.mult, ALU.mult
                                                   ).then_inc(mid_ready.sem, 1)
                for b in two:
                    evacuate_x(i + b + 2, b)
                    dve.wait_ge(down_done.sem, down_done.part(i + b, 1))
                    dve.wait_ge(y_out[b].sem, 8 * i + 16)
                    nc.vector.tensor_copy(y[b][:, 0:512], ps[:, 5, :]).then_inc(y_vec.sem, 1)

        @block.tensor
        def _(pe):
            mm, tr = nc.tensor.matmul, nc.tensor.transpose

            def turn(j, b, x_count):
                pe.wait_ge(x_in[b], x_count)
                for a in range(2):
                    pe.wait_ge(xt_act.sem if a else xt_vec.sem, xt_vec.back(j, 1))
                    for c in range(4):
                        t = tr(ps[:, a, c * P:(c + 1) * P], x[b][:, (4 * a + c) * P:(4 * a + c + 1) * P], ident[:])
                    t.then_inc(turned.sem, 1)

            total = n_blocks(pe)
            turn(0, 0, 16)
            turn(1, 1, 16)
            with pe.Fori(0, total, 2) as i:
                for b in two:
                    pe.wait_ge(xt_vec.sem, xt_vec.all(i + b))
                    pe.wait_ge(xt_act.sem, xt_act.all(i + b))
                    pe.wait_ge(mid_ready.sem, mid_ready.back(i + b, 2))
                    pe.wait_ge(gate_in[b].sem, 8 * i + 32)
                    pe.wait_ge(up_in[b].sem, 8 * i + 32)
                    for c in range(KC):
                        t = mm(ps[:, 2 + b, :], xt[b][:, c, :], w_gu[b][:, :, c, :], start=(c == 0), stop=(c == KC - 1))
                    t.then_inc(gu_done.sem, 1)
                for b in two:
                    pe.wait_ge(mid_ready.sem, mid_ready.all(i + b))
                    pe.wait_ge(midt_ready.sem, midt_ready.back(i + b, 1))
                    for c in range(FC):
                        t = tr(ps[:, 4, c * P:(c + 1) * P],
                               mid[b][:].rearrange("p (q c) -> p c q", c=FC)[:, c, :], ident[:])
                    t.then_inc(midt_turned.sem, 1)
                    turn(i + b + 2, b, 8 * i + 32)
                    pe.wait_ge(midt_ready.sem, midt_ready.all(i + b))
                    pe.wait_ge(down_in[b].sem, 8 * i + 32)
                    for n in range(2):
                        pe.wait_ge(y_act.sem if n else y_vec.sem, y_vec.back(i + b, 1))
                        for c in range(FC):
                            t = mm(ps[:, 5 + n, :], midt[b][:, c, :], w_dn[b][:, c, n * 512:(n + 1) * 512],
                                   start=(c == 0), stop=(c == FC - 1))
                        t.then_inc(down_done.sem, 1)


def combine(nc, A, S, O):
    ys = O["y_sample"].rearrange("b t d -> (b t) d")
    with Phase(nc, "p7_") as ctx:
        sb, sem = ctx.sb, ctx.sem
        signals = []

        def signal(name, n=1, ahead=1):
            signals.append(Signal(sem(name), n, ahead))
            return signals[-1]

        two = range(2)
        gain, half = sb("gain", [P, D]), sb("half", [P, 2 * H])
        h = [sb(f"h{b}", [P, D]) for b in two]
        dest = [sb(f"dest{b}", [P, 2], I32) for b in two]
        w = [sb(f"w{b}", [P, 2]) for b in two]
        ya = [[sb(f"y{k}{b}", [P, D]) for b in two] for k in range(2)]
        sq = sb("sq", [P, D])
        ss, ms, rs = ([sb(f"{n}{b}", [P, 1]) for b in two] for n in ("ss", "ms", "rs"))
        out = [sb(f"out{b}", [P, D]) for b in two]
        consts_in = sem("consts_in")
        h_in, dest_in, w_in, stored = ([signal(f"{n}{b}", 16) for b in two] for n in (
            "h_in", "dest_in", "w_in", "stored"))
        gathered = [sem(f"gathered{b}") for b in two]
        vec_own, summed, squared, pool_own, rs_ready, out_ready = (signal(n, 1, 2) for n in (
            "vec_own", "summed", "squared", "pool_own", "rs_ready", "out_ready"))
        block = ctx.block()

        @block.sync
        def _(sp):
            for sig in signals:
                sp.sem_inc(sig.sem, sig.n * sig.ahead)
            sp.dma_start(gain[:], A["norm_final"].unsqueeze(0).to_broadcast([P, D])).then_inc(consts_in, 16)
            sp.dma_start(half[:], A["c_half"]).then_inc(consts_in, 16)

            def load(j, b):
                sp.wait_ge(out_ready.sem, out_ready.back(j, 2))
                sp.dma_start(dest[b][:], rows(S["dest"], j)).then_inc(dest_in[b].sem, 16)
                sp.dma_start(w[b][:], rows(S["weights"], j)).then_inc(w_in[b].sem, 16)
                sp.dma_start(h[b][:], rows(S["h"], j)).then_inc(h_in[b].sem, 16)

            with sp.Fori(0, NT - 1, 2) as i:
                for b in two:
                    load(i + b, b)
            sp.wait_ge(out_ready.sem, out_ready.back(NT, 2))
            sp.dma_start(dest[0][0:NS], rows(S["dest"], NT, NS)).then_inc(dest_in[0].sem, 16)
            sp.dma_start(w[0][0:NS], rows(S["weights"], NT, NS)).then_inc(w_in[0].sem, 16)
            sp.dma_start(h[0][0:NS], rows(S["h"], NT, NS)).then_inc(h_in[0].sem, 16)

        @block.gpsimd
        def _(pool):
            pool.wait_ge(consts_in, 32)

            def fetch(j, b, k2, r):
                pool.wait_ge(dest_in[b].sem, 8 * k2 + 32)
                pool.wait_ge(summed.sem, summed.back(j, 2))
                apart(pool, consts_in, 32)
                for k in range(2):
                    pool.indirect_dma_start(out=ya[k][b][0:r], out_offset=None, in_=S["y"],
                                            in_offset=bass.IndirectOffsetOnAxis(ap=dest[b][0:r, k:k + 1], axis=0)
                                            ).then_inc(gathered[b], 16)

            def root(j, b):
                pool.wait_ge(squared.sem, squared.all(j))
                apart(pool, consts_in, 32)
                nc.gpsimd.tensor_scalar(ms[b][:], ss[b][:], 1.0 / D, EPS, ALU.mult, ALU.add).then_inc(pool_own.sem, 1)
                pool.wait_ge(pool_own.sem, pool_own.all(j))
                nc.gpsimd.tensor_tensor(rs[b][:], ms[b][:], half[:, 0:1], ALU.pow).then_inc(rs_ready.sem, 1)

            fetch(0, 0, 0, P)
            fetch(1, 1, 0, P)
            with pool.Fori(0, NT - 3, 2) as i:
                for b in two:
                    root(i + b, b)
                    fetch(i + b + 2, b, i + 2, P)
            root(NT - 2, 0)
            fetch(NT, 0, NT, NS)
            root(NT - 1, 1)
            root(NT, 0)

        @block.scalar
        def _(act):
            def square(j, b):
                act.wait_ge(summed.sem, summed.all(j))
                act.wait_ge(rs_ready.sem, rs_ready.back(j, 2))
                act.wait_ge(squared.sem, squared.back(j, 1))
                nc.scalar.activation(sq[:], out[b][:], ACT.Square, accum_out=ss[b][:]).then_inc(squared.sem, 1)

            def store(dst, j, b, r=P):
                act.wait_ge(out_ready.sem, out_ready.all(j))
                act.dma_start(dst, out[b][0:r]).then_inc(stored[b].sem, 16)

            yp = O["y_prompt"][0]
            with act.Fori(0, NT - 1, 2) as i:
                for b in two:
                    square(i + b, b)
                for b in two:
                    store(rows(yp, i + b), i + b, b)
            square(NT, 0)
            store(ys, NT, 0, NS)
            act.wait_ge(stored[0].sem, stored[0].all(NT // 2))
            act.wait_ge(stored[1].sem, stored[1].all(NT // 2 - 1))

        @block.vector
        def _(dve):
            dve.wait_ge(consts_in, 32)

            def add(j, b, k2):
                dve.wait_ge(h_in[b].sem, 8 * k2 + 32)
                dve.wait_ge(w_in[b].sem, 8 * k2 + 32)
                dve.wait_ge(gathered[b], 16 * k2 + 32)
                dve.wait_ge(stored[b].sem, 8 * k2 + 16)
                nc.vector.scalar_tensor_tensor(out[b][:], ya[0][b][:], w[b][:, 0:1], h[b][:], ALU.mult, ALU.add
                                               ).then_inc(vec_own.sem, 1)
                dve.wait_ge(vec_own.sem, vec_own.all(j))
                nc.vector.scalar_tensor_tensor(out[b][:], ya[1][b][:], w[b][:, 1:2], out[b][:], ALU.mult, ALU.add
                                               ).then_inc(summed.sem, 1)

            def scale(j, b):
                dve.wait_ge(rs_ready.sem, rs_ready.all(j))
                nc.vector.scalar_tensor_tensor(out[b][:], out[b][:], rs[b][:], gain[:], ALU.mult, ALU.mult
                                               ).then_inc(out_ready.sem, 1)

            with dve.Fori(0, NT - 1, 2) as i:
                for b in two:
                    add(i + b, b, i)
                for b in two:
                    scale(i + b, b)
            add(NT, 0, NT)
            scale(NT, 0)


def scratch(nc):
    def dram(name, shape, dt=F32):
        return nc.dram_tensor("s_" + name, shape, dt).ap()

    return {
        "qkv": dram("qkv", (TILES * P, QKV)),
        "zab": dram("zab", (TILES * P, ZAB)),
        "conv_p": dram("conv_p", (SEQ + CW - 1, CC)),
        "conv_s": dram("conv_s", (DB * (DT + CW - 1), CC)),
        "gb": dram("gb", (TILES * P, 2 * H)),
        "swa_s": dram("swa_s", (NS, H * HD)),
        "h": dram("h", (NTOK, D)),
        "hn": dram("hn", (NTOK, D)),
        "logits": dram("logits", (TILES * P, NR)),
        "slots": dram("slots", (SLOT_BLOCKS * P, 1), I32),
        "owner": dram("owner", (1, MAXB + 2), I32),
        "dest": dram("dest", (TILES * P, 2), I32),
        "weights": dram("weights", (TILES * P, 2)),
        "y": dram("y", ((MINB + ZFILL * (NT // 2 - 1)) * P, D)),
    }




def build(nc, A, O):
    S = scratch(nc)
    project_in(nc, A, S)
    token_gates(nc, A, S)
    mix_prompt(nc, A, S, O)
    mix_samples(nc, A, S, O)
    route(nc, A, S)
    experts(nc, A, S)
    combine(nc, A, S, O)


_INS = ["x_prompt", "x_sample", "cache_swa_k", "cache_swa_v", "state_gdn_conv", "state_gdn", "norm_mix", "w_in",
        "swa_sinks", "gdn_conv_w", "gdn_A_log", "gdn_dt_bias", "gdn_norm_w", "w_out", "norm_ffn",
        "w_router_group", "b_router_group", "w_router_expert", "b_router_expert",
        "w_exp_gate", "w_exp_up", "w_exp_down", "norm_final"]
_OUTS = {"y_prompt": (1, SEQ, D), "y_sample": (DB, DT, D),
         "k_prompt": (1, 1, W, KVH, HD), "v_prompt": (1, 1, W, KVH, HD),
         "k_sample": (1, DB, W, KVH, HD), "v_sample": (1, DB, W, KVH, HD),
         "conv_prompt": (1, 1, CW - 1, CC), "conv_sample": (1, DB, CW - 1, CC),
         "gdn_prompt": (1, 1, H, HD, HD), "gdn_sample": (1, DB, H, HD, HD)}


def kernel(**inputs):
    import concourse.bacc as _bacc
    from concourse.bass_utils import run_bass_kernel_spmd as _run

    nc = _bacc.Bacc("TRN2", target_bir_lowering=False, num_devices=1)
    arrays, A, O = {}, {}, {}
    named = {n: np.ascontiguousarray(inputs[n]) for n in _INS}
    named["sink_rows"] = np.ascontiguousarray(
        np.broadcast_to(named["swa_sinks"].reshape(1, H, 1), (2, H, DT)).reshape(P, 1))
    named.update({"c_" + k: v for k, v in constants().items()})
    for name, a in named.items():
        arrays[f"in_{name}"] = a
        A[name] = nc.dram_tensor(f"in_{name}", a.shape, mybir.dt.from_np(a.dtype), kind="ExternalInput").ap()
    for name, shape in _OUTS.items():
        O[name] = nc.dram_tensor(f"out_{name}", shape, F32, kind="ExternalOutput").ap()
    build(nc, A, O)
    r = _run(nc, [arrays], core_ids=[0])
    return tuple(r.results[0][f"out_{name}"] for name in _OUTS)
```
